# Optimizing a Trainium2 kernel written in Bass

```python
import jax, jax.numpy as jnp
from jax import lax
import numpy as np

D_MODEL = 2048
BATCH = 1
SEQ = 256
DEPTH = 1

PLE_DIM = 256
EPS = 1e-6
CONV_CH = D_MODEL // 4
CONV_WIDTH = 31
GLA_HEADS = 4
GLA_DV = D_MODEL // 16
GLA_DK = GLA_DV // 2
GLA_GATE_RANK = 16
GLA_TAU = 16.0
GLA_CHUNK = 64
MOBA_HEADS = 8
MOBA_HD = D_MODEL // 16
MOBA_BLOCK = 256
MOBA_TOPK = 3
MOBA_Q_CHUNK = 64
N_BRANCH = 3
FFN_DIM = ((8 * D_MODEL // 3 + 255) // 256) * 256
FFN_CONV_WIDTH = 3
IN_SIZES = (2 * CONV_CH,
            GLA_HEADS * GLA_DK,
            GLA_HEADS * GLA_DK,
            GLA_HEADS * GLA_DV,
            GLA_HEADS * GLA_DV,
            GLA_GATE_RANK,
            MOBA_HEADS * MOBA_HD,
            MOBA_HEADS * MOBA_HD,
            MOBA_HEADS * MOBA_HD)
IN_COLS = sum(IN_SIZES)

kernel_name = "hybrid_conformer_gla_moba_block"

def rms_norm(x, g):
    xf = x.astype(jnp.float32)
    y = xf * lax.rsqrt(jnp.mean(xf * xf, axis=-1, keepdims=True) + EPS)
    return (y * g.astype(jnp.float32)).astype(x.dtype)

def layer_norm(x, g, b):
    xf = x.astype(jnp.float32)
    mu = jnp.mean(xf, axis=-1, keepdims=True)
    xc = xf - mu
    y = xc * lax.rsqrt(jnp.mean(xc * xc, axis=-1, keepdims=True) + EPS)
    return (y * g.astype(jnp.float32) + b.astype(jnp.float32)).astype(x.dtype)

def causal_dwconv(x, w):
    k_w = w.shape[0]
    s = x.shape[1]
    xp = jnp.pad(x, ((0, 0), (k_w - 1, 0), (0, 0)))
    out = xp[:, k_w - 1:k_w - 1 + s] * w[k_w - 1]
    for j in range(k_w - 1):
        out = out + xp[:, j:j + s] * w[j]
    return out

def conformer_conv_branch(z_glu, conv_w, conv_b, ln_g, ln_b, w_o):
    val, gate = jnp.split(z_glu, 2, axis=-1)
    a = val * jax.nn.sigmoid(gate)
    a = causal_dwconv(a, conv_w) + conv_b
    a = jax.nn.silu(layer_norm(a, ln_g, ln_b))
    return a @ w_o

def gla_branch(q, k, v, r, a_low, w_a2, b_a, norm_g, w_o):
    b_sz, s, _ = q.shape
    n_c = s // GLA_CHUNK
    q = q.reshape(b_sz, s, GLA_HEADS, GLA_DK) * (GLA_DK ** -0.5)
    k = k.reshape(b_sz, s, GLA_HEADS, GLA_DK)
    v = v.reshape(b_sz, s, GLA_HEADS, GLA_DV)
    log_a = jax.nn.log_sigmoid((a_low @ w_a2 + b_a).astype(jnp.float32)) / GLA_TAU
    log_a = log_a.reshape(b_sz, s, GLA_HEADS, GLA_DK)

    def to_chunks(t):
        return t.reshape(b_sz, n_c, GLA_CHUNK, GLA_HEADS, -1).transpose(1, 0, 3, 2, 4).astype(jnp.float32)

    tri = jnp.tril(jnp.ones((GLA_CHUNK, GLA_CHUNK), dtype=bool))

    def step(state, xs):
        qc, kc, vc, lac = xs
        bc = jnp.cumsum(lac, axis=2)
        inter = jnp.einsum('bhtd,bhde->bhte', qc * jnp.exp(bc), state)
        diff = bc[:, :, :, None, :] - bc[:, :, None, :, :]
        decay = jnp.exp(jnp.where(tri[None, None, :, :, None], diff, -jnp.inf))
        attn = jnp.einsum('bhtd,bhsd,bhtsd->bhts', qc, kc, decay)
        intra = jnp.einsum('bhts,bhse->bhte', attn, vc)
        b_last = bc[:, :, -1, :]
        k_dec = kc * jnp.exp(b_last[:, :, None, :] - bc)
        state = state * jnp.exp(b_last)[..., None] + jnp.einsum('bhsd,bhse->bhde', k_dec, vc)
        return state, inter + intra

    state0 = jnp.zeros((b_sz, GLA_HEADS, GLA_DK, GLA_DV), jnp.float32)
    _, o = lax.scan(step, state0, (to_chunks(q), to_chunks(k), to_chunks(v), to_chunks(log_a)))
    o = o.transpose(1, 0, 3, 2, 4).reshape(b_sz, s, GLA_HEADS, GLA_DV).astype(v.dtype)
    o = rms_norm(o, norm_g) * jax.nn.silu(r.reshape(b_sz, s, GLA_HEADS, GLA_DV))
    return o.reshape(b_sz, s, GLA_HEADS * GLA_DV) @ w_o

def moba_branch(q, k, v, q_norm_g, k_norm_g, w_o):
    b_sz, s, _ = q.shape
    q = rms_norm(q.reshape(b_sz, s, MOBA_HEADS, MOBA_HD), q_norm_g).transpose(0, 2, 1, 3)
    k = rms_norm(k.reshape(b_sz, s, MOBA_HEADS, MOBA_HD), k_norm_g).transpose(0, 2, 1, 3)
    v = v.reshape(b_sz, s, MOBA_HEADS, MOBA_HD).transpose(0, 2, 1, 3)
    s_pad = -(-s // MOBA_BLOCK) * MOBA_BLOCK
    pad = ((0, 0), (0, 0), (0, s_pad - s), (0, 0))
    q, k, v = jnp.pad(q, pad), jnp.pad(k, pad), jnp.pad(v, pad)
    n_blk = s_pad // MOBA_BLOCK
    top_k = min(MOBA_TOPK, n_blk)
    kb = k.reshape(b_sz, MOBA_HEADS, n_blk, MOBA_BLOCK, MOBA_HD)
    vb = v.reshape(b_sz, MOBA_HEADS, n_blk, MOBA_BLOCK, MOBA_HD)
    k_mean = jnp.mean(kb.astype(jnp.float32), axis=3)
    n_q = s_pad // MOBA_Q_CHUNK
    q_chunks = q.reshape(b_sz, MOBA_HEADS, n_q, MOBA_Q_CHUNK, MOBA_HD).transpose(2, 0, 1, 3, 4)
    b_idx = jnp.arange(b_sz)[:, None, None, None]
    h_idx = jnp.arange(MOBA_HEADS)[None, :, None, None]
    scale = MOBA_HD ** -0.5

    def chunk(args):
        c, qc = args
        q_pos = c * MOBA_Q_CHUNK + jnp.arange(MOBA_Q_CHUNK)
        q_blk = q_pos // MOBA_BLOCK
        blk_s = jnp.einsum('bhqd,bhnd->bhqn', qc.astype(jnp.float32), k_mean)
        past = jnp.arange(n_blk)[None, :] < q_blk[:, None]
        blk_s = jnp.where(past, blk_s, -jnp.inf)
        top_val, top_idx = lax.top_k(blk_s, top_k)
        sel_ok = jnp.isfinite(top_val)
        k_sel = kb[b_idx, h_idx, top_idx]
        v_sel = vb[b_idx, h_idx, top_idx]
        s_sel = jnp.einsum('bhqd,bhqjkd->bhqjk', qc, k_sel).astype(jnp.float32) * scale
        s_sel = jnp.where(sel_ok[..., None], s_sel, -jnp.inf)
        s_sel = s_sel.reshape(b_sz, MOBA_HEADS, MOBA_Q_CHUNK, top_k * MOBA_BLOCK)
        own_start = (c * MOBA_Q_CHUNK // MOBA_BLOCK) * MOBA_BLOCK
        k_own = lax.dynamic_slice_in_dim(k, own_start, MOBA_BLOCK, axis=2)
        v_own = lax.dynamic_slice_in_dim(v, own_start, MOBA_BLOCK, axis=2)
        s_own = jnp.einsum('bhqd,bhkd->bhqk', qc, k_own).astype(jnp.float32) * scale
        k_pos = own_start + jnp.arange(MOBA_BLOCK)
        s_own = jnp.where(k_pos[None, :] <= q_pos[:, None], s_own, -jnp.inf)
        probs = jax.nn.softmax(jnp.concatenate([s_sel, s_own], axis=-1), axis=-1).astype(v.dtype)
        p_sel = probs[..., :top_k * MOBA_BLOCK].reshape(b_sz, MOBA_HEADS, MOBA_Q_CHUNK, top_k, MOBA_BLOCK)
        p_own = probs[..., top_k * MOBA_BLOCK:]
        return (jnp.einsum('bhqjk,bhqjkd->bhqd', p_sel, v_sel)
                + jnp.einsum('bhqk,bhkd->bhqd', p_own, v_own))

    o = lax.map(chunk, (jnp.arange(n_q), q_chunks))
    o = o.transpose(1, 0, 3, 2, 4).reshape(b_sz, s_pad, MOBA_HEADS * MOBA_HD)[:, :s]
    return o @ w_o

def setup_inputs(seed: int = 0) -> dict:
    key = jax.random.key(seed)
    ks = jax.random.split(key, 32)
    L, D, F = DEPTH, D_MODEL, FFN_DIM

    def w(k, shape, fan_in):
        return jax.random.normal(k, shape, jnp.float32) * (fan_in ** -0.5)

    def gain(k, shape):
        return 1.0 + 0.05 * jax.random.normal(k, shape, jnp.float32)

    def bias(k, shape):
        return 0.01 * jax.random.normal(k, shape, jnp.float32)

    return {
        "x": jax.random.normal(ks[0], (BATCH, SEQ, D), jnp.float32),
        "p": jax.random.normal(ks[1], (DEPTH, BATCH, SEQ, PLE_DIM), jnp.float32),
        "norm_mix_g": gain(ks[2], (L, D)),
        "w_in": w(ks[3], (L, D, IN_COLS), D),
        "conv_w": w(ks[4], (L, CONV_WIDTH, CONV_CH), CONV_WIDTH),
        "conv_b": bias(ks[5], (L, CONV_CH)),
        "conv_ln_g": gain(ks[6], (L, CONV_CH)),
        "conv_ln_b": bias(ks[7], (L, CONV_CH)),
        "w_conv_out": w(ks[8], (L, CONV_CH, D), CONV_CH),
        "gla_w_a2": w(ks[9], (L, GLA_GATE_RANK, GLA_HEADS * GLA_DK), GLA_GATE_RANK),
        "gla_b_a": bias(ks[10], (L, GLA_HEADS * GLA_DK)),
        "gla_norm_g": gain(ks[11], (L, GLA_DV)),
        "w_gla_out": w(ks[12], (L, GLA_HEADS * GLA_DV, D), GLA_HEADS * GLA_DV),
        "moba_q_norm_g": gain(ks[13], (L, MOBA_HD)),
        "moba_k_norm_g": gain(ks[14], (L, MOBA_HD)),
        "w_moba_out": w(ks[15], (L, MOBA_HEADS * MOBA_HD, D), MOBA_HEADS * MOBA_HD),
        "w_gate": w(ks[16], (L, D, N_BRANCH * D), D),
        "b_gate": bias(ks[17], (L, N_BRANCH * D)),
        "w_out": w(ks[18], (L, D, D), D),
        "norm_ffn_g": gain(ks[19], (L, D)),
        "w_up": w(ks[20], (L, D, 2 * F), D),
        "ffn_conv_w": w(ks[21], (L, FFN_CONV_WIDTH, 2 * F), FFN_CONV_WIDTH),
        "w_down": w(ks[22], (L, F, D), F),
        "norm_ple_g": gain(ks[23], (L, D)),
        "w_ple_gate": w(ks[24], (L, D, D), D),
        "w_ple": w(ks[25], (L, PLE_DIM, D), PLE_DIM),
    }

def reference(x, p, norm_mix_g, w_in, conv_w, conv_b, conv_ln_g, conv_ln_b, w_conv_out,
              gla_w_a2, gla_b_a, gla_norm_g, w_gla_out, moba_q_norm_g, moba_k_norm_g, w_moba_out,
              w_gate, b_gate, w_out, norm_ffn_g, w_up, ffn_conv_w, w_down,
              norm_ple_g, w_ple_gate, w_ple):
    b_sz, s, d = x.shape
    offsets = np.cumsum(IN_SIZES)[:-1].tolist()
    for i in range(DEPTH):
        h = rms_norm(x, norm_mix_g[i])
        z = h @ w_in[i]
        z_glu, gq, gk, gv, gr, ga, mq, mk, mv = jnp.split(z, offsets, axis=-1)
        y_a = conformer_conv_branch(z_glu, conv_w[i], conv_b[i], conv_ln_g[i], conv_ln_b[i], w_conv_out[i])
        y_b = gla_branch(gq, gk, gv, gr, ga, gla_w_a2[i], gla_b_a[i], gla_norm_g[i], w_gla_out[i])
        y_c = moba_branch(mq, mk, mv, moba_q_norm_g[i], moba_k_norm_g[i], w_moba_out[i])
        gates = jax.nn.sigmoid(h @ w_gate[i] + b_gate[i]).reshape(b_sz, s, N_BRANCH, d)
        merged = gates[:, :, 0] * y_a + gates[:, :, 1] * y_b + gates[:, :, 2] * y_c
        x = x + merged @ w_out[i]
        h = rms_norm(x, norm_ffn_g[i])
        u = causal_dwconv(h @ w_up[i], ffn_conv_w[i])
        u_g, u_v = jnp.split(u, 2, axis=-1)
        x = x + (jax.nn.silu(u_g) * u_v) @ w_down[i]
        g = jax.nn.sigmoid(rms_norm(x, norm_ple_g[i]) @ w_ple_gate[i])
        x = x + g * (p[i] @ w_ple[i])
    return x


_drawn_inputs = setup_inputs


def setup_inputs(seed=0):
    import zlib

    import numpy as np

    out = dict(_drawn_inputs(seed))
    spreads = {}
    factors = {'conv_b': 8.0,
     'conv_ln_g': 3.001,
     'conv_ln_b': 27.555,
     'gla_b_a': 22.222,
     'gla_norm_g': 3.374,
     'moba_q_norm_g': 8.0,
     'moba_k_norm_g': 8.0,
     'b_gate': 8.0,
     'norm_ple_g': 26.56}
    for name, (base, spread) in spreads.items():
        noise = np.random.default_rng([zlib.crc32(name.encode()), seed]).standard_normal(out[name].shape)
        drawn = base * np.exp(spread * noise) if base else spread * noise
        out[name] = __import__('jax').numpy.asarray(drawn.astype(out[name].dtype))
    for name, factor in factors.items():
        out[name] = (out[name] * factor).astype(out[name].dtype)
    return out
```

```python
from contextlib import ExitStack

import numpy as np

import concourse.bass as bass
from concourse import mybir

F32 = mybir.dt.float32
F32R = mybir.dt.float32r
ALU = mybir.AluOpType
ACT = mybir.ActivationFunctionType
AX_X = mybir.AxisListType.X

P = 128
D = 2048
S = 256
TT = S // P
KD = D // P
EPS = 1e-6
CONV_CH = D // 4
TAPS = 31
GLA_HEADS, GLA_DK, GLA_DV, GLA_RANK, GLA_TAU, GLA_CHUNK = 4, 64, 128, 16, 16.0, 64
HEADS, HD = 8, 128
PLE = 256
FFN = 5632
FT = FFN // P
FFN_TAPS = 3

RING = 4
W = 512
CH = 1024
QD = 4

C_VAL, C_GATE, C_QK, C_GV, C_GR, C_GA, C_MQ, C_MK, C_MV = 0, 512, 1024, 1536, 2048, 2560, 2576, 3600, 4624

GROUPS = []


def _plan():
    c = 0
    for name, count, chunks in (("val", 1, 8), ("gate", 1, 8), ("qk", 1, 8), ("alow", 1, 2),
                                ("gv", 1, 8), ("gr", 1, 8), ("mq", 1, 8), ("mk", 1, 8),
                                ("mq2", 1, 8), ("mk2", 1, 8), ("mv", 2, 8), ("yA", 4, 2),
                                ("gA", 4, 8), ("yB", 4, 2), ("gB", 4, 8), ("yC", 4, 4),
                                ("gC", 4, 8), ("wout", 4, 8), ("ple", 4, 1)):
        for g in range(count):
            GROUPS.append((name, g, c, chunks))
            c += chunks
    return c


UP1 = _plan()
PAIRS1, PAIRS2 = 6, 5
K1, K2 = PAIRS1 * QD, PAIRS2 * QD
DOWN1 = UP1 + 16 * PAIRS1
UP2 = DOWN1 + 4 * K1 // 2
DOWN2 = UP2 + 16 * PAIRS2
PLEG = DOWN2 + 4 * K2 // 2
END = PLEG + 32
GROUP_AT = {}
for _n, (_name, _g, _c0, _k) in enumerate(GROUPS):
    for _j in range(_k):
        GROUP_AT[_c0 + _j] = (_name, _g, _j, _k, _n)
FIRST = {(name, g): c0 for name, g, c0, _ in GROUPS}
LAST = {(name, g): c0 + k - 1 for name, g, c0, k in GROUPS}
NUMBER = {(name, g): n for n, (name, g, _, _) in enumerate(GROUPS)}
N_STRAIGHT = len(GROUPS)

U_H, U_A, U_B, U_C, U_P, U_M, U_X1, U_F, U_X2 = 0, 4, 5, 6, 14, 15, 19, 23, 34

R_MIX, R_CB, R_LG, R_LB, R_GLA, R_Q, R_K, R_BG, R_FFN, R_PLE, R_ALL = 0, 16, 20, 24, 28, 29, 30, 31, 79, 95, 111

MASKED = -1e30


def trunk(nc, x, p, norm_mix_g, w_in, conv_w, conv_b, conv_ln_g, conv_ln_b, w_conv_out,
          gla_w_a2, gla_b_a, gla_norm_g, w_gla_out, moba_q_norm_g, moba_k_norm_g, w_moba_out,
          w_gate, b_gate, w_out, norm_ffn_g, w_up, ffn_conv_w, w_down,
          norm_ple_g, w_ple_gate, w_ple, out):
    base = (nc.sbuf_base + 31) // 32 * 32
    KB = 1024
    top = [base]

    def at(name, shape, dtype, offset):
        return nc.alloc_sbuf_tensor_at(name, shape, dtype, offset=offset)

    def new(name, shape, dtype=F32):
        n = 4 * int(np.prod(shape[1:]))
        t = at(name, shape, dtype, top[0])
        top[0] += (n + 31) // 32 * 32
        return t

    raw = new("raw", [P, RING, CH])
    w_hi = new("w_hi", [P, RING, CH], F32R)
    w_lo = new("w_lo", [P, RING, CH], F32R)
    h_hi = new("h_hi", [P, KD, S], F32R)
    h_lo = new("h_lo", [P, KD, S], F32R)
    xT = new("xT", [P, KD, S])
    full = new("full", [P, 2, QD, S])
    ms = new("ms", [P, 8])
    par = new("par", [P, R_ALL])
    parh = new("parh", [P, R_ALL])
    cw = new("cw", [P, TAPS * QD])
    fw = new("fw", [P, FFN_TAPS, 2 * FT])
    ident = new("ident", [P, P])
    ones = new("ones", [P, P])
    tri = new("tri", [P, P])
    cmask = new("cmask", [P, 3, P])
    rq = new("rq", [P, 2, 8])
    rB = new("rB", [P, S])
    small = new("small", [P, 16])
    arena = top[0]
    assert arena + 90 * KB <= nc.sbuf_usable_end, (arena, nc.sbuf_usable_end)

    def ar(name, shape, kb, dtype=F32):
        return at(name, shape, dtype, arena + int(kb * KB))

    xtok = ar("xtok", [P, TT, D], 0)
    junk = ar("junk", [P, 4 * TT, W], 48)
    pst = ar("pst", [P, 6, P], 32)
    val = ar("val", [P, QD, S], 0)
    tanhg = ar("tanhg", [P, QD, S], 4)
    apad = ar("apad", [P, QD, TAPS - 1 + S], 8)
    a_hi = ar("a_hi", [P, QD, S], 16, F32R)
    a_lo = ar("a_lo", [P, QD, S], 20, F32R)
    sqm = ar("sqm", [P, QD, S], 24)
    masks = ar("masks", [P, 7, P], 28)
    merged = ar("merged", [P, KD, S], 0)
    yb = ar("yb", [P, KD, S], 16)
    mq = ar("mq", [P, HEADS, S], 32)
    mk = ar("mk", [P, HEADS, S], 40)
    mv = ar("mv", [P, TT, HEADS * HD], 48)
    gqk = ar("gqk", [P, 4 * S], 56)
    gv = ar("gv", [P, TT, W], 60)
    gr = ar("gr", [P, QD, S], 64)
    bc = ar("bc", [P, 2 * S], 68)
    ex = ar("ex", [P, 2 * S], 70)
    lqk = ar("lqk", [P, 4 * S], 72)
    alow = ar("alow", [GLA_RANK, S], 72)
    wa2 = ar("wa2", [GLA_RANK, S], 73)
    brow = ar("brow", [1, S], 74)
    att = ar("att", [P, GLA_HEADS, 3, P], 76)
    tmpg = ar("tmpg", [P, QD * S], 82)
    gt = ar("gt", [P, QD, S], 86)
    o_hi = ar("o_hi", [P, QD, S], 68, F32R)
    o_lo = ar("o_lo", [P, QD, S], 72, F32R)
    c_hi = ar("c_hi", [P, HEADS, S], 56, F32R)
    c_lo = ar("c_lo", [P, HEADS, S], 64, F32R)
    sc = ar("sc", [P, 2, 3 * P], 72)
    pT = ar("pT", [P, 2, 3 * P], 78)
    m_hi = ar("m_hi", [P, KD, S], 32, F32R)
    m_lo = ar("m_lo", [P, KD, S], 48, F32R)
    p_hi = ar("p_hi", [P, 2, S], 64, F32R)
    p_lo = ar("p_lo", [P, 2, S], 66, F32R)
    ptok = ar("ptok", [P, TT, PLE], 82)
    sqx = ar("sqx", [P, QD, S], 0)
    sqsum = ar("sqsum", [P, QD, S], 4)
    upg = ar("upg", [P, QD, 2 + S], 0)
    upv = ar("upv", [P, QD, 2 + S], 4.25)
    cg = ar("cg", [P, QD, S], 8.5)
    cv = ar("cv", [P, QD, S], 12.5)
    tg = ar("tg", [P, QD, S], 16.5)
    f_hi = ar("f_hi", [P, K1, S], 20.5, F32R)
    f_lo = ar("f_lo", [P, K1, S], 44.5, F32R)
    ple = ar("ple", [P, TT, D], 68.5)
    x2tok = ar("x2tok", [P, TT, D], 20.5)
    gt2 = ar("gt2", [P, TT, W], 8.5)
    fin = ar("fin", [P, 2, TT, W], 36.5)

    acc = [nc.alloc_psum_tensor(f"acc{i}", [P, QD, S], F32) for i in range(2)]
    fa = nc.alloc_psum_tensor("fa", [P, 2, 512], F32)
    fb = nc.alloc_psum_tensor("fb", [P, 2, 512], F32)

    def flat(t):
        return t[:].rearrange("p a b -> p (a b)")

    def sem(name):
        return nc.alloc_semaphore(name)

    chunk_landed = [sem(f"chunk_landed{i}") for i in range(RING)]
    chunk_high, chunk_split, chunk_used = sem("chunk_high"), sem("chunk_split"), sem("chunk_used")
    taken = [sem("taken0"), sem("taken1")]
    unit_full, unit_high, unit_split = sem("unit_full"), sem("unit_high"), sem("unit_split")
    x_landed = [sem(f"x_landed{q}") for q in range(4)]
    gain_landed, par_landed, p_landed = sem("gain_landed"), sem("par_landed"), sem("p_landed")
    out_landed = [sem("out_landed0"), sem("out_landed1")]
    consts = sem("consts")
    ms_ready, rs_ready = sem("ms_ready"), sem("rs_ready")
    gain_turned, gain_ready, par_turned, par_ready = (
        sem(n) for n in ("gain_turned", "gain_ready", "par_turned", "par_ready"))
    ssq_ready = sem("ssq_ready")
    xq_turned, xq_taken = sem("xq_turned"), sem("xq_taken")
    rs_spread, rb_ready = sem("rs_spread"), sem("rb_ready")
    act_step, dve_step, pool_step = sem("act_step"), sem("dve_step"), sem("pool_step")
    la_sums, la_abs, la_exp, la_ready = sem("la_sums"), sem("la_abs"), sem("la_exp"), sem("la_ready")
    bc_sums, bc_ready = sem("bc_sums"), sem("bc_ready")
    conv_ready, mean_sums, xc_ready, xcsq_ready, var_sums, yh_ready, ytanh_ready = (
        sem(n) for n in ("conv_ready", "mean_sums", "xc_ready", "xcsq_ready", "var_sums", "yh_ready", "ytanh_ready"))
    norm_sums, qk_normed = sem("norm_sums"), sem("qk_normed")
    exps_wanted, exps_ready, level_ready, level_sums, att_ready = (
        sem(n) for n in ("exps_wanted", "exps_ready", "level_ready", "level_sums", "att_ready"))
    gla_o, gla_osq, gla_oss, gla_r = sem("gla_o"), sem("gla_osq"), sem("gla_oss"), sem("gla_r")
    sc_sums, sc_ready, sc_exp, pr_ready, pr_turned, pT_ready, pv_sums = (
        sem(n) for n in ("sc_sums", "sc_ready", "sc_exp", "pr_ready", "pr_turned", "pT_ready", "pv_sums"))
    gate_ready, gate_merged = sem("gate_ready"), sem("gate_merged")
    p_turned = sem("p_turned")
    x_new, xsq_ready, xsum_ready, xss = sem("x_new"), sem("xsq_ready"), sem("xsum_ready"), sem("xss")
    tap_ready, cg_ready, tg_ready = sem("tap_ready"), sem("cg_ready"), sem("tg_ready")
    x2_turned, x2_taken = sem("x2_turned"), sem("x2_taken")
    r2_ready, pg_ready, out_ready = sem("r2_ready"), sem("pg_ready"), sem("out_ready")
    cv_ready = sem("cv_ready")

    def unit_dst(u):
        if u < U_A:
            return h_hi[:, 4 * u:4 * u + 4, :], h_lo[:, 4 * u:4 * u + 4, :], 4
        if u == U_A:
            return a_hi[:], a_lo[:], 4
        if u == U_B:
            return o_hi[:], o_lo[:], 4
        if u < U_P:
            return c_hi[:, u - U_C:u - U_C + 1, :], c_lo[:, u - U_C:u - U_C + 1, :], 1
        if u == U_P:
            return p_hi[:], p_lo[:], 2
        if u < U_X1:
            k = 4 * (u - U_M)
            return m_hi[:, k:k + 4, :], m_lo[:, k:k + 4, :], 4
        k = 4 * (u - U_X1)
        return h_hi[:, k:k + 4, :], h_lo[:, k:k + 4, :], 4

    def wait_taken(eng, n):
        eng.wait_ge(taken[n % 2], n // 2 + 1)

    NG_UP1 = N_STRAIGHT
    NG_DOWN1 = NG_UP1 + 2 * PAIRS1
    NG_UP2 = NG_DOWN1 + 4
    NG_DOWN2 = NG_UP2 + 2 * PAIRS2
    NG_PLEG = NG_DOWN2 + 4
    assert NG_UP1 % 2 == 0

    rows = [(norm_mix_g[0], R_MIX), (conv_b[0], R_CB), (conv_ln_g[0], R_LG), (conv_ln_b[0], R_LB),
            (gla_norm_g[0], R_GLA), (moba_q_norm_g[0], R_Q), (moba_k_norm_g[0], R_K), (b_gate[0], R_BG),
            (norm_ffn_g[0], R_FFN), (norm_ple_g[0], R_PLE)]
    par_dmas = len(rows) + 1 + FFN_TAPS + 2

    block = nc.Block()
    block.__enter__()

    @block.sync
    def _(sp):
        def chunk(c, src, k, i=None, step=0):
            if i is not None:
                sp.wait_ge(chunk_split, i * step + (c - RING + 1))
            elif c >= RING:
                sp.wait_ge(chunk_split, c - RING + 1)
            sp.dma_start(raw[:, c % RING, :].rearrange("p (k n) -> p k n", k=k),
                         src.rearrange("(k p) n -> p k n", p=P)).then_inc(chunk_landed[c % RING], 16)

        for q in range(4):
            sp.dma_start(xtok[:, :, q * W:(q + 1) * W],
                         x[0, :, q * W:(q + 1) * W].rearrange("(t p) n -> p t n", p=P)).then_inc(x_landed[q], 16)
        wi, wg = w_in[0], w_gate[0]
        cols = {"val": C_VAL, "gate": C_GATE, "qk": C_QK, "gv": C_GV, "gr": C_GR, "mq": C_MQ,
                "mk": C_MK, "mq2": C_MQ + W, "mk2": C_MK + W}
        for name, g, c0, n in GROUPS:
            if name == "gB" and g == 1:
                sp.wait_ge(chunk_used, FIRST["gB", 0])
                sp.dma_start(ptok[:], p[0, 0].rearrange("(t p) n -> p t n", p=P)).then_inc(p_landed, 16)
            for j in range(n):
                c = c0 + j
                if name in cols:
                    chunk(c, wi[j * 256:(j + 1) * 256, cols[name]:cols[name] + W], 2)
                elif name == "alow":
                    chunk(c, wi[j * 1024:(j + 1) * 1024, C_GA:C_GA + P], 8)
                elif name == "mv":
                    chunk(c, wi[j * 256:(j + 1) * 256, C_MV + g * W:C_MV + (g + 1) * W], 2)
                elif name in ("gA", "gB", "gC"):
                    col = "ABC".index(name[1]) * D + g * W
                    chunk(c, wg[j * 256:(j + 1) * 256, col:col + W], 2)
                else:
                    w = {"yA": w_conv_out, "yB": w_gla_out, "yC": w_moba_out, "wout": w_out, "ple": w_ple}[name][0]
                    chunk(c, w[j * 256:(j + 1) * 256, g * W:(g + 1) * W], 2)

        def up(c0, pairs, pair0):
            with sp.Fori(0, pairs) as i:
                for part in range(2):
                    for j in range(8):
                        chunk(c0 + 8 * part + j,
                              w_up[0][j * 256:(j + 1) * 256, bass.ds(i * W + (part * FFN + pair0 * W), W)],
                              2, i, 16)

        def down(c0, kt, kt0):
            n = kt // 2
            with sp.Fori(0, 2) as i:
                for half in range(2):
                    for j in range(n):
                        chunk(c0 + half * n + j,
                              w_down[0][(kt0 + 2 * j) * P:(kt0 + 2 * j + 2) * P, bass.ds(i * 2 * W + half * W, W)],
                              2, i, 2 * n)

        up(UP1, PAIRS1, 0)
        down(DOWN1, K1, 0)
        up(UP2, PAIRS2, PAIRS1)
        down(DOWN2, K2, K1)
        with sp.Fori(0, 2) as i:
            for half in range(2):
                for j in range(8):
                    chunk(PLEG + 8 * half + j,
                          w_ple_gate[0][j * 256:(j + 1) * 256, bass.ds(i * 2 * W + half * W, W)], 2, i, 16)
        for g in range(4):
            sp.wait_ge(out_ready, g + 1)
            for t in range(TT):
                sp.dma_start(out[0, t * P:(t + 1) * P, g * W:(g + 1) * W], fin[:, g % 2, t, :]).then_inc(out_landed[g % 2], 16)
        for s in range(2):
            sp.wait_ge(out_landed[s], 16 * 2 * TT)

    @block.gpsimd
    def _(pool):
        nc.gpsimd.memset(ones[:], 1.0).then_inc(pool_step, 1)
        nc.gpsimd.memset(small[:, 15:16], -0.5).then_inc(pool_step, 1)
        pool.wait_ge(pool_step, 2)
        nc.gpsimd.affine_select(out=ident[:], in_=ones[:], compare_op=ALU.is_equal, fill=0.0, base=0,
                                pattern=[[-1, P]], channel_multiplier=1).then_inc(consts, 1)
        def rsqrt(n, cols):
            pool.wait_ge(ms_ready, n)
            nc.gpsimd.tensor_tensor(ms[:, 0:cols], ms[:, 0:cols], small[:, 15:16].to_broadcast([P, cols]),
                                    ALU.pow).then_inc(rs_ready, 1)

        n = 2
        nc.gpsimd.memset(cmask[:], 0.0).then_inc(pool_step, 1)
        n += 1
        pool.wait_ge(pool_step, n)
        for b in (0, 2):
            nc.gpsimd.affine_select(out=cmask[:, b, :], in_=cmask[:, b, :], compare_op=ALU.is_ge, fill=MASKED,
                                    base=0, pattern=[[-1, P]], channel_multiplier=1).then_inc(pool_step, 1)
            n += 1
        rsqrt(1, TT)
        for v, r in rows:
            pool.dma_start(pst[r:r + v.shape[0] // P, 0, :], v.rearrange("(r p) -> r p", p=P)).then_inc(par_landed, 16)
        pool.dma_start(pst[0:TAPS * QD, 1, :], conv_w[0].rearrange("w (j p) -> (w j) p", p=P)).then_inc(par_landed, 16)
        for k in range(FFN_TAPS):
            pool.dma_start(pst[0:2 * FT, 2 + k, :], ffn_conv_w[0, k].rearrange("(r p) -> r p", p=P)).then_inc(par_landed, 16)
        pool.dma_start(wa2[:], gla_w_a2[0]).then_inc(par_landed, 16)
        pool.dma_start(brow[:], gla_b_a).then_inc(par_landed, 16)
        nc.gpsimd.memset(tri[:], 1.0 / GLA_TAU).then_inc(pool_step, 1)
        n += 1
        pool.wait_ge(pool_step, n)
        blocks = tri[:].rearrange("p (b n) -> p b n", n=GLA_CHUNK)
        nc.gpsimd.affine_select(out=blocks, in_=blocks, compare_op=ALU.is_ge, fill=0.0, base=0,
                                pattern=[[-GLA_CHUNK, P // GLA_CHUNK], [0, GLA_CHUNK]],
                                channel_multiplier=1).then_inc(pool_step, 1)
        n += 1
        pool.wait_ge(pool_step, n)
        nc.gpsimd.affine_select(out=tri[:], in_=tri[:], compare_op=ALU.is_ge, fill=0.0, base=0,
                                pattern=[[1, P]], channel_multiplier=-1).then_inc(pool_step, 1)
        n += 1
        nc.gpsimd.memset(masks[:], 1.0).then_inc(pool_step, 1)
        n += 1
        for i in range(7):
            half = 1 << i
            v = masks[:, i, :].rearrange("p (b two n) -> p b two n", two=2, n=half)
            whole = masks[:, i, :].rearrange("p (b n) -> p b n", n=2 * half)
            pool.wait_ge(pool_step, n)
            nc.gpsimd.affine_select(out=whole, in_=whole, compare_op=ALU.is_ge, fill=0.0, base=0,
                                    pattern=[[-2 * half, P // (2 * half)], [0, 2 * half]],
                                    channel_multiplier=1).then_inc(pool_step, 1)
            n += 1
            pool.wait_ge(pool_step, n)
            nc.gpsimd.affine_select(out=whole, in_=whole, compare_op=ALU.is_ge, fill=0.0, base=half - 1,
                                    pattern=[[2 * half, P // (2 * half)], [0, 2 * half]],
                                    channel_multiplier=-1).then_inc(pool_step, 1)
            n += 1
            pool.wait_ge(pool_step, n)
            last = nc.gpsimd.memset(v[:, :, 0, :], 0.0)
            last.then_inc(pool_step if i < 6 else consts, 1)
            n += 1
        for k, cols in enumerate((8, TT, 8, 8, 8, 8, TT, TT)):
            rsqrt(2 + k, cols)

    @block.tensor
    def _(pe):
        def products(dst, stat_hi, stat_lo, mov_hi, mov_lo, first, last):
            nc.tensor.matmul(dst, stat_hi, mov_hi, start=first, stop=False, skip_group_check=True)
            nc.tensor.matmul(dst, stat_hi, mov_lo, start=False, stop=False, skip_group_check=True)
            return nc.tensor.matmul(dst, stat_lo, mov_hi, start=False, stop=last, skip_group_check=True)

        def feature_chunk(c, s, a_h, a_l, kt, first, last, i=None, step=0):
            pe.wait_ge(chunk_split, c + 1 if i is None else i * step + (c + 1))
            for k in range(2):
                for j in range(QD):
                    w = slice(k * W + j * P, k * W + (j + 1) * P)
                    mm = products(acc[s][:, j, :], w_hi[:, c % RING, w], w_lo[:, c % RING, w],
                                  a_h[:, kt + k, :], a_l[:, kt + k, :],
                                  first and k == 0 and j % 2 == 0, last and k == 1)
            mm.then_inc(chunk_used, 1)

        def token_chunk(c, s, a_h, a_l, kt, first, last, i=None, step=0):
            pe.wait_ge(chunk_split, c + 1 if i is None else i * step + (c + 1))
            dst = flat(acc[s])
            for k in range(2):
                for t in range(TT):
                    o = dst[:, t * W:(t + 1) * W]
                    w = slice(k * W, (k + 1) * W)
                    sh, sl = a_h[:, kt + k, t * P:(t + 1) * P], a_l[:, kt + k, t * P:(t + 1) * P]
                    nc.tensor.matmul(o, sh, w_hi[:, c % RING, w], start=first and k == 0, stop=False, skip_group_check=True)
                    nc.tensor.matmul(o, sh, w_lo[:, c % RING, w], start=False, stop=False, skip_group_check=True)
                    mm = nc.tensor.matmul(o, sl, w_hi[:, c % RING, w], start=False, stop=last and k == 1, skip_group_check=True)
            mm.then_inc(chunk_used, 1)

        def column_sums(dst, src, n, k):
            for j in range(k):
                mm = nc.tensor.matmul(dst, ones[:], src[:, j, :n], start=j == 0, stop=j == k - 1, skip_group_check=True)
            return mm

        def token_sums(dst, src):
            for j in range(QD):
                for t in range(TT):
                    mm = nc.tensor.matmul(dst[:, 2 * j + t:2 * j + t + 1], src[:, j, t * P:(t + 1) * P], ones[:, 0:1],
                                          start=True, stop=True, skip_group_check=True)
            return mm

        def token_total(dst, src):
            for t in range(TT):
                for j in range(QD):
                    mm = nc.tensor.matmul(dst[:, t:t + 1], src[:, j, t * P:(t + 1) * P], ones[:, 0:1],
                                          start=j == 0, stop=j == QD - 1, skip_group_check=True)
            return mm

        def spread(n, dst, k):
            pe.wait_ge(rs_ready, n)
            for j in range(k):
                for t in range(TT):
                    i_ = 2 * j + t
                    mm = nc.tensor.matmul(dst[:, i_ * P:(i_ + 1) * P], ms[:, i_:i_ + 1].broadcast_to([P, P]), ident[:],
                                          start=True, stop=True, skip_group_check=True)
            mm.then_inc(rs_spread, 1)

        fa_flat = fa[:].rearrange("p b n -> p (b n)")
        fb_flat = fb[:].rearrange("p b n -> p (b n)")

        pe.wait_ge(consts, 1)
        pe.wait_ge(gain_landed, 16)
        nc.tensor.transpose(acc[0][:, 0, 0:KD], pst[0:KD, 5, :], ident[0:KD, 0:KD]).then_inc(gain_turned, 1)
        for q in range(4):
            dst = (fa if q % 2 == 0 else fb)[:].rearrange("p b (j s) -> p (b j) s", j=2)
            pe.wait_ge(x_landed[q], 16)
            if q >= 2:
                pe.wait_ge(xq_taken, q - 1)
            for j in range(QD):
                for t in range(TT):
                    k = 4 * q + j
                    mm = nc.tensor.transpose(dst[:, j, t * P:(t + 1) * P], xtok[:, t, k * P:(k + 1) * P], ident[:])
            mm.then_inc(xq_turned, 1)
        spread(1, flat(acc[1]), 1)

        levels = {66: 0}
        levels.update({71 + 4 * n: n for n in range(1, 9)})

        def gla_level(n):
            if n == 0:
                wait_taken(pe, NUMBER["qk", 0])
                pe.wait_ge(yh_ready, 1)
                q, k = gqk[:, 0:2 * S], gqk[:, 2 * S:4 * S]
            else:
                pe.wait_ge(level_ready, n)
                q, k = lqk[:, 0:2 * S], lqk[:, 2 * S:4 * S]
            for par_ in range(2):
                r = slice(64 * par_, 64 * par_ + 64)
                for hp in range(2):
                    if n < 8:
                        for t in range(TT):
                            w = slice(hp * S + t * P, hp * S + (t + 1) * P)
                            mm = nc.tensor.matmul(fb[:, par_, (2 * hp + t) * P:(2 * hp + t + 1) * P], k[r, w], q[r, w],
                                                  start=True, stop=True, skip_group_check=True)
                    else:
                        mm = nc.tensor.matmul(fb[:, par_, hp * P:(hp + 1) * P], k[r, hp * S:hp * S + P],
                                              q[r, hp * S + P:hp * S + S], start=True, stop=True, skip_group_check=True)
            mm.then_inc(level_sums, 1)

        def scores(h):
            if h == 0:
                pe.wait_ge(qk_normed, 4)
                pe.wait_ge(unit_full, U_B + 1)
                pe.wait_ge(gla_r, 1)
            if h >= 2:
                pe.wait_ge(sc_ready, h - 1)
            nc.tensor.matmul(fa[:, h % 2, P:3 * P], mq[:, h, P:S], mk[:, h, :], start=True, stop=True, skip_group_check=True)
            nc.tensor.matmul(fa[:, h % 2, 0:P], mq[:, h, 0:P], mk[:, h, 0:P], start=True, stop=True,
                             skip_group_check=True).then_inc(sc_sums, 1)

        def turn_probs(h):
            pe.wait_ge(pr_ready, h + 1)
            if h >= 1:
                pe.wait_ge(pT_ready, h)
            for b in range(3):
                mm = nc.tensor.transpose(fb[:, 0, b * P:(b + 1) * P], sc[:, h % 2, b * P:(b + 1) * P], ident[:])
            mm.then_inc(pr_turned, 1)

        def probs_v(h):
            pe.wait_ge(pT_ready, h + 1)
            if h == 0:
                for n in (0, 1):
                    wait_taken(pe, NUMBER["mv", n])
            else:
                pe.wait_ge(unit_full, U_C + h)
            nc.tensor.matmul(fb[:, 1, 0:S], mv[:, 0, h * HD:(h + 1) * HD], pT[:, h % 2, 0:S], start=True, stop=False, skip_group_check=True)
            nc.tensor.matmul(fb[:, 1, P:S], mv[:, 1, h * HD:(h + 1) * HD], pT[:, h % 2, S:S + P], start=False, stop=True,
                             skip_group_check=True).then_inc(pv_sums, 1)

        gb0 = FIRST["gB", 0]
        for c in range(UP1):
            name, g, j, n, number = GROUP_AT[c]
            s = number % 2
            if j == 0:
                if c == 0:
                    pe.wait_ge(gain_ready, 1)
                if c == FIRST["gate", 0]:
                    pe.wait_ge(rb_ready, 1)
                if number >= 2:
                    wait_taken(pe, number - 2)
            first, last = j == 0, j == n - 1
            if name in ("val", "gate", "qk", "gr", "mq", "mk", "mq2", "mk2", "gA", "gB", "gC"):
                if c < 8 and j % 2 == 0:
                    pe.wait_ge(unit_split, U_H + j // 2 + 1)
                feature_chunk(c, s, h_hi, h_lo, 2 * j, first, last)
            elif name in ("gv", "mv"):
                token_chunk(c, s, h_hi, h_lo, 2 * j, first, last)
            elif name == "alow":
                pe.wait_ge(chunk_split, c + 1)
                for k in range(8):
                    w = slice(k * P, (k + 1) * P)
                    mm = products(acc[s][:, 0, :], w_hi[:, c % RING, w], w_lo[:, c % RING, w], h_hi[:, 8 * j + k, :],
                                  h_lo[:, 8 * j + k, :], first and k == 0, last and k == 7)
                mm.then_inc(chunk_used, 1)
            elif name == "yA":
                pe.wait_ge(unit_split, U_A + 1)
                feature_chunk(c, s, a_hi, a_lo, 2 * j, first, last)
            elif name == "yB":
                pe.wait_ge(unit_split, U_B + 1)
                feature_chunk(c, s, o_hi, o_lo, 2 * j, first, last)
            elif name == "yC":
                pe.wait_ge(unit_split, U_C + 2 * j + 2)
                feature_chunk(c, s, c_hi, c_lo, 2 * j, first, last)
            elif name == "wout":
                pe.wait_ge(unit_split, U_M + j // 2 + 1)
                feature_chunk(c, s, m_hi, m_lo, 2 * j, first, last)
            elif name == "ple":
                token_chunk(c, s, p_hi, p_lo, 0, True, True)

            if c == 10:
                pe.wait_ge(par_landed, 16 * par_dmas)
                pe.wait_ge(xq_taken, 4)
                for b, n_rows in enumerate((R_ALL, TAPS * QD, 2 * FT, 2 * FT, 2 * FT)):
                    mm = nc.tensor.transpose(fb_flat[:, b * P:b * P + n_rows], pst[0:n_rows, b, :], ident[0:n_rows, 0:n_rows])
                mm.then_inc(par_turned, 1)
            if c == 28:
                wait_taken(pe, NUMBER["alow", 0])
                pe.wait_ge(par_ready, 1)
                for t in range(TT):
                    nc.tensor.matmul(fb[:, t, 0:S], alow[:, t * P:(t + 1) * P], wa2[:], start=True, stop=False, skip_group_check=True)
                    mm = nc.tensor.matmul(fb[:, t, 0:S], ones[0:1, :], brow[:], start=False, stop=True, skip_group_check=True)
                mm.then_inc(la_sums, 1)
            if c == 36:
                pe.wait_ge(la_ready, 1)
                pe.wait_ge(consts, 2)
                for hp in range(2):
                    for t in range(TT):
                        mm = nc.tensor.matmul(fb[:, 0, hp * S + t * P:hp * S + (t + 1) * P],
                                              ex[:, t * S + hp * P:t * S + (hp + 1) * P], tri[:], start=True, stop=True, skip_group_check=True)
                mm.then_inc(bc_sums, 1)
            if c == 52:
                pe.wait_ge(conv_ready, 1)
                pe.wait_ge(bc_ready, 1)
                column_sums(fb[:, 0, 0:S], val, S, QD).then_inc(mean_sums, 1)
            if c == 58:
                pe.wait_ge(xcsq_ready, 1)
                token_total(fb[:, 1, :], tanhg).then_inc(var_sums, 1)
            if c == 60:
                spread(3, fb[:, 1, :], 1)
            for k, name_ in enumerate(("mq", "mk", "mq2", "mk2")):
                if c == LAST[name_, 0] + 6:
                    wait_taken(pe, NUMBER[name_, 0])
                    if k:
                        pe.wait_ge(qk_normed, k)
                    token_sums(fa_flat, sqm).then_inc(norm_sums, 1)
                if c == LAST[name_, 0] + 8 and k % 2:
                    spread((4, 6)[k // 2], fa_flat, 4)
            if c in levels:
                gla_level(levels[c])
            if c == 108:
                pe.wait_ge(att_ready, 1)
                pe.wait_ge(qk_normed, 4)
                for h in range(GLA_HEADS):
                    a = 2 * (h % 2) + h // 2
                    o = slice((h % 2) * S, (h % 2) * S + S)
                    nc.tensor.matmul(fa[:, h // 2, o], gv[:, 0, h * P:(h + 1) * P], att[:, a, 0:2, :].rearrange("p a b -> p (a b)"),
                                     start=h % 2 == 0, stop=False, skip_group_check=True)
                    mm = nc.tensor.matmul(fa[:, h // 2, o.start + P:o.stop], gv[:, 1, h * P:(h + 1) * P], att[:, a, 2, :],
                                          start=False, stop=True, skip_group_check=True)
                mm.then_inc(gla_o, 1)
            if c == 113:
                pe.wait_ge(gla_osq, 1)
                token_sums(fb_flat, tmpg[:].rearrange("p (j s) -> p j s", j=QD)).then_inc(gla_oss, 1)
            if c == 115:
                spread(7, fb_flat, 4)
            i = c - gb0
            if 0 <= i < 33:
                if i % 4 == 0 and i:
                    probs_v(i // 4 - 1)
                if i % 4 == 0 and i < 32:
                    scores(i // 4)
                if i % 4 == 3:
                    turn_probs(i // 4)
            if c == FIRST["gC", 0] + 4:
                pe.wait_ge(p_landed, 16)
                pe.wait_ge(sc_ready, HEADS)
                for k in range(2):
                    for t in range(TT):
                        mm = nc.tensor.transpose(fa[:, 0, k * S + t * P:k * S + (t + 1) * P], ptok[:, t, k * P:(k + 1) * P], ident[:])
                mm.then_inc(p_turned, 1)
        pe.wait_ge(xsum_ready, 4)
        pe.wait_ge(unit_full, U_P + 1)
        token_total(fa_flat, sqsum).then_inc(xss, 1)
        spread(8, fa_flat, 1)

        def up(c0, pairs, group0, u_first):
            with pe.Fori(0, pairs) as i:
                for part in range(2):
                    pe.wait_ge(taken[part], i + group0 // 2)
                    for j in range(8):
                        if part == 0 and u_first and j % 2 == 0:
                            pe.wait_ge(unit_split, U_X1 + j // 2 + 1)
                        feature_chunk(c0 + 8 * part + j, part, h_hi, h_lo, 2 * j, j == 0, j == 7, i, 16)

        def down(c0, kt, group0, u0):
            n = kt // 2
            with pe.Fori(0, 2) as i:
                for half in range(2):
                    pe.wait_ge(taken[half], i + group0 // 2)
                    for j in range(n):
                        if half == 0 and j % 2 == 0:
                            pe.wait_ge(unit_split, u0 + j // 2 + 1)
                        feature_chunk(c0 + half * n + j, half, f_hi, f_lo, 2 * j, j == 0, j == n - 1, i, 2 * n)

        up(UP1, PAIRS1, NG_UP1, True)
        down(DOWN1, K1, NG_DOWN1, U_F)
        up(UP2, PAIRS2, NG_UP2, False)
        down(DOWN2, K2, NG_DOWN2, U_F + PAIRS1)
        for g in range(4):
            number = NG_PLEG + g
            wait_taken(pe, number - 2)
            for j in range(8):
                c = PLEG + 8 * g + j
                if g == 0 and j % 2 == 0:
                    pe.wait_ge(unit_split, U_X2 + j // 2 + 1)
                token_chunk(c, number % 2, h_hi, h_lo, 2 * j, j == 0, j == 7)
                if g == 1 and j < 4:
                    if j == 1:
                        pe.wait_ge(ms_ready, 9)
                    if j >= 2:
                        pe.wait_ge(x2_taken, j - 1)
                    dst = fb if j % 2 == 0 else fa
                    for t in range(TT):
                        for k in range(QD):
                            mm = nc.tensor.transpose(dst[:, t, k * P:(k + 1) * P], xT[:, 4 * j + k, t * P:(t + 1) * P], ident[:])
                    mm.then_inc(x2_turned, 1)
            if g == 0:
                pe.wait_ge(xsum_ready, 8)
                token_total(fa_flat, sqsum).then_inc(xss, 1)


    @block.scalar
    def _(act):
        A = nc.scalar
        act.dma_start(pst[0:KD, 5, :], norm_mix_g[0].rearrange("(r p) -> r p", p=P)).then_inc(gain_landed, 16)

        highs = [0]

        def earlier():
            act.wait_ge(chunk_high, highs[0])

        def high(c, i=None, step=0):
            highs[0] = c + 1 if i is None else i * step + (c + 1)
            if i is None:
                act.wait_ge(chunk_landed[c % RING], 16 * (c // RING + 1))
                if c >= RING:
                    act.wait_ge(chunk_used, c - RING + 1)
            else:
                act.wait_ge(chunk_landed[c % RING], i * (16 * step // RING) + 16 * (c // RING + 1))
                act.wait_ge(chunk_used, i * step + (c - RING + 1))
            A.copy(w_hi[:, c % RING, :], raw[:, c % RING, :]).then_inc(chunk_high, 1)

        def unit_to_high(u, src, dst, need=None):
            act.wait_ge(unit_full, u + 1 if need is None else need)
            A.copy(dst, src).then_inc(unit_high, 1)

        def unit(u):
            hi, _, n = unit_dst(u)
            unit_to_high(u, full[:, u % 2, 0:n, :], hi)

        act.wait_ge(consts, 1)
        A.activation(rB[:, 0:P], ones[:], ACT.Tanh).then_inc(act_step, 1)
        for q in range(4):
            act.wait_ge(x_landed[q], 16)
            for t in range(TT):
                last = A.activation(junk[:, 2 * q + t, :], xtok[:, t, q * W:(q + 1) * W], ACT.Square,
                                    accum_out=small[:, 4 * t + q:4 * t + q + 1])
        last.then_inc(ssq_ready, 1)
        for c in range(4):
            high(c)
            unit(U_H + c)

        def take(number, dst, src, scale=None):
            if scale is None:
                return A.copy(dst, src).then_inc(taken[number % 2], 1)
            return A.mul(dst, src, scale).then_inc(taken[number % 2], 1)

        gb0 = FIRST["gB", 0]
        for c in range(4, UP1 + 12):
            high(c)
            e = c - RING
            if e in GROUP_AT and e == LAST[GROUP_AT[e][:2]]:
                earlier()
                name, g, _, _, number = GROUP_AT[e]
                a = acc[number % 2]
                if name == "val":
                    act.wait_ge(unit_split, U_H + 4)
                    take(number, val[:], a[:], 0.5)
                elif name == "gate":
                    A.activation(tanhg[:], a[:], ACT.Tanh, scale=0.5).then_inc(taken[number % 2], 1)
                elif name == "qk":
                    A.mul(gqk[:, 0:2 * S], flat(a)[:, 0:2 * S], GLA_DK ** -0.5)
                    take(number, gqk[:, 2 * S:4 * S], flat(a)[:, 2 * S:4 * S])
                elif name == "alow":
                    take(number, alow[:], a[0:GLA_RANK, 0, :])
                elif name == "gv":
                    take(number, flat(gv), flat(a))
                elif name == "gr":
                    A.activation(tmpg[:], flat(a), ACT.Tanh, scale=0.5)
                    take(number, gr[:], a[:], 0.5)
                elif name in ("mq", "mk", "mq2", "mk2"):
                    k = ("mq", "mk", "mq2", "mk2").index(name)
                    dst = (mq, mk)[k % 2]
                    A.mul(dst[:, 4 * (k // 2):4 * (k // 2) + 4, :], a[:], par[:, R_Q + k % 2:R_Q + k % 2 + 1])
                    if k:
                        act.wait_ge(norm_sums, k)
                    A.activation(sqm[:], a[:], ACT.Square).then_inc(taken[number % 2], 1)
                elif name == "mv":
                    take(number, mv[:, :, g * W:(g + 1) * W], flat(a).rearrange("p (t n) -> p t n", t=TT))
                elif name == "yA":
                    take(number, merged[:, 4 * g:4 * g + 4, :], a[:], 0.5)
                elif name in ("yB", "yC"):
                    if name == "yB" and g == 0:
                        act.wait_ge(att_ready, 1)
                    if name == "yC":
                        act.wait_ge(gate_merged, 4 + g + 1)
                    take(number, yb[:, 4 * g:4 * g + 4, :], a[:], 0.5)
                elif name in ("gA", "gB", "gC"):
                    b = "ABC".index(name[1])
                    if b == 2 and g:
                        act.wait_ge(unit_full, U_M + g)
                    elif 4 * b + g:
                        act.wait_ge(gate_merged, 4 * b + g)
                    for j in range(QD):
                        col = R_BG + 16 * b + 4 * g + j
                        last = A.activation(gt[:, j, :], a[:, j, :], ACT.Tanh, bias=parh[:, col:col + 1], scale=0.5)
                    last.then_inc(taken[number % 2], 1)
                elif name == "ple":
                    take(number, ple[:, :, g * W:(g + 1) * W], flat(a).rearrange("p (t n) -> p t n", t=TT), 0.5)
            if c == 33:
                earlier()
                act.wait_ge(la_abs, 1)
                A.activation(lqk[:, 0:2 * S], lqk[:, 0:2 * S], ACT.Exp, scale=-1.0).then_inc(act_step, 1)
                act.wait_ge(act_step, 2)
                A.activation(lqk[:, 0:2 * S], lqk[:, 0:2 * S], ACT.Ln, bias=1.0).then_inc(la_exp, 1)
            if c == 40:
                earlier()
                act.wait_ge(bc_sums, 1)
                A.copy(bc[:], fb[:, 0, :]).then_inc(bc_ready, 1)
            if c == 57:
                earlier()
                act.wait_ge(xc_ready, 1)
                A.activation(tanhg[:], val[:], ACT.Square).then_inc(xcsq_ready, 1)
            if c == 66:
                earlier()
                act.wait_ge(yh_ready, 1)
                A.activation(tanhg[:], val[:], ACT.Tanh).then_inc(ytanh_ready, 1)
            if c == 69:
                earlier()
                unit(U_A)
            for n in range(1, 9):
                if c == 72 + 4 * n:
                    earlier()
                    act.wait_ge(exps_wanted, n)
                    A.activation(ex[:], ex[:], ACT.Exp).then_inc(exps_ready, 1)
            if c == 112:
                earlier()
                act.wait_ge(gla_o, 1)
                A.activation(tmpg[:], fa[:].rearrange("p b n -> p (b n)"), ACT.Square).then_inc(gla_osq, 1)
            if c == 120:
                earlier()
                unit(U_B)
            i = c - gb0
            if 0 <= i < 38:
                earlier()
                if i % 4 == 3 and i // 4 < HEADS:
                    h = i // 4
                    act.wait_ge(sc_ready, h + 1)
                    b = 2 + 6 * (h % 2)
                    for t, w in ((0, slice(0, P)), (1, slice(P, 3 * P))):
                        last = A.activation(sc[:, h % 2, w], sc[:, h % 2, w], ACT.Exp, bias=small[:, b + t:b + t + 1],
                                            scale=rq[:, h // 4, 2 * (h % 4) + t:2 * (h % 4) + t + 1],
                                            accum_out=small[:, b + 2 + t:b + 3 + t])
                    last.then_inc(sc_exp, 1)
                if i % 4 == 2 and i >= 6:
                    h = (i - 6) // 4
                    act.wait_ge(pr_turned, h + 1)
                    if h >= 2:
                        act.wait_ge(pv_sums, h - 1)
                    A.copy(pT[:, h % 2, :], fb[:, 0, 0:3 * P]).then_inc(pT_ready, 1)
                if i % 4 == 0 and i >= 8:
                    unit(U_C + i // 4 - 2)
            if c == FIRST["gC", 0] + 9:
                earlier()
                unit(U_P)
            for g in range(4):
                if c == LAST["gC", g] + 5:
                    earlier()
                    unit(U_M + g)
                if c == LAST["wout", g] + 5:
                    earlier()
                    unit(U_X1 + g)
                    act.wait_ge(x_new, g + 1)
                    if g:
                        act.wait_ge(xsum_ready, g)
                    A.activation(sqx[:], xT[:, 4 * g:4 * g + 4, :], ACT.Square).then_inc(xsq_ready, 1)

        def taps0(k, src, dst, col, need, i):
            act.wait_ge(taken[k], need)
            earlier()
            for j in range(QD):
                last = A.mul(dst[:, j, :], src[:, j, 2:2 + S], fw[:, 2, bass.ds(i * QD + (col + j), 1)])
            last.then_inc(tap_ready, 1)

        def up(c0, pairs, group0, pair0, u0, tap0):
            with act.Fori(0, pairs) as i:
                highs[0] = i * 16 + (c0 + 12)
                taps0(0, upg, cg, 4 * pair0, i + (group0 // 2 + 1), i)
                for k in range(12, 15):
                    high(c0 + k, i, 16)
                act.wait_ge(cg_ready, i + (pair0 + 1))
                earlier()
                A.activation(tg[:], cg[:], ACT.Tanh).then_inc(tg_ready, 1)
                for k in range(15, 20):
                    high(c0 + k, i, 16)
                taps0(1, upv, cv, FT + 4 * pair0, i + (group0 // 2 + 1), i)
                for k in range(20, 23):
                    high(c0 + k, i, 16)
                earlier()
                unit_to_high(0, full[:, 0, :, :], f_hi[:, bass.ds(i * QD, QD), :], need=i + (u0 + 1))
                for k in range(23, 28):
                    high(c0 + k, i, 16)

        def down(c0, kt):
            n = kt // 2
            with act.Fori(0, 2) as i:
                for k in range(12, 12 + 2 * n):
                    high(c0 + k, i, 2 * n)

        up(UP1, PAIRS1, NG_UP1, 0, U_F, 0)
        down(DOWN1, K1)
        up(UP2, PAIRS2, NG_UP2, PAIRS1, U_F + PAIRS1, 0)
        n = K2 // 2
        with act.Fori(0, 2) as i:
            for k in range(12, 12 + 2 * n):
                high(DOWN2 + k, i, 2 * n)
                for half in range(2):
                    if k == half * n + n + 4:
                        earlier()
                        unit_to_high(0, full[:, half, :, :], h_hi[:, bass.ds(i * 8 + 4 * half, 4), :],
                                     need=i * 2 + (U_X2 + half + 1))
                        act.wait_ge(xsum_ready, i * 2 + (4 + half))
                        A.activation(sqx[:], xT[:, bass.ds(i * 8 + 4 * half, 4), :], ACT.Square).then_inc(xsq_ready, 1)
        for c in range(PLEG + 12, END + 4):
            if c < END:
                high(c)
            earlier()
            q = c - PLEG - 12
            if q < 4:
                act.wait_ge(x2_turned, q + 1)
                A.copy(x2tok[:, :, q * W:(q + 1) * W], (fb if q % 2 == 0 else fa)[:]).then_inc(x2_taken, 1)
            for g in range(4):
                if c == PLEG + 8 * g + (13 if g == 0 else 11):
                    number = NG_PLEG + g
                    act.wait_ge(chunk_used, PLEG + 8 * g + 8)
                    act.wait_ge(r2_ready, 1)
                    if g:
                        act.wait_ge(pg_ready, g)
                    for t in range(TT):
                        last = A.activation(gt2[:, t, :], flat(acc[number % 2])[:, t * W:(t + 1) * W], ACT.Tanh,
                                            scale=small[:, 14 - t:15 - t])
                    last.then_inc(taken[number % 2], 1)

    @block.vector
    def _(dve):
        V = nc.vector
        steps = [0]

        def step(ins):
            ins.then_inc(dve_step, 1)
            steps[0] += 1

        def sync():
            dve.wait_ge(dve_step, steps[0])

        splits = [0]

        def earlier():
            dve.wait_ge(chunk_split, splits[0])

        def split(c, i=None, step=0):
            splits[0] = c + 1 if i is None else i * step + (c + 1)
            dve.wait_ge(chunk_high, c + 1 if i is None else i * step + (c + 1))
            V.tensor_tensor(w_lo[:, c % RING, :], raw[:, c % RING, :], w_hi[:, c % RING, :].bitcast(F32),
                            ALU.subtract).then_inc(chunk_split, 1)

        def unit(u):
            hi, lo, n = unit_dst(u)
            dve.wait_ge(unit_high, u + 1)
            V.tensor_tensor(lo, full[:, u % 2, 0:n, :], hi.bitcast(F32), ALU.subtract).then_inc(unit_split, 1)

        def quad(a):
            return a.unsqueeze(1).broadcast_to([P, QD, S])

        dve.wait_ge(gain_turned, 1)
        V.tensor_copy(par[:, 0:KD], acc[0][:, 0, 0:KD]).then_inc(gain_ready, 1)
        for q in range(4):
            dve.wait_ge(xq_turned, q + 1)
            V.tensor_copy(xT[:, 4 * q:4 * q + 4, :].rearrange("p j s -> p (j s)"),
                          (fa if q % 2 == 0 else fb)[:].rearrange("p b n -> p (b n)")).then_inc(xq_taken, 1)
        dve.wait_ge(ssq_ready, 1)
        step(V.tensor_reduce(ms[:, 0:TT], small[:, 0:4 * TT].rearrange("p (t q) -> p t q", t=TT), AX_X, ALU.add))
        sync()
        V.tensor_scalar(ms[:, 0:TT], ms[:, 0:TT], 1.0 / D, EPS, ALU.mult, ALU.add).then_inc(ms_ready, 1)
        dve.wait_ge(rs_spread, 1)
        V.tensor_copy(rB[:], acc[1][:, 0, :]).then_inc(rb_ready, 1)
        dve.wait_ge(rb_ready, 1)
        dve.wait_ge(xq_taken, 4)
        dve.wait_ge(gain_ready, 1)
        for q in range(5):
            if q < 4:
                if q >= 2:
                    dve.wait_ge(unit_split, q - 1)
                for j in range(QD):
                    k = 4 * q + j
                    last = V.scalar_tensor_tensor(full[:, q % 2, j, :], xT[:, k, :], par[:, R_MIX + k:R_MIX + k + 1],
                                                  rB[:], ALU.mult, ALU.mult)
                last.then_inc(unit_full, 1)
            if q:
                split(q - 1)
                unit(U_H + q - 1)

        def glu():
            wait_taken(dve, NUMBER["val", 0])
            wait_taken(dve, NUMBER["gate", 0])
            V.memset(apad[:, :, 0:TAPS - 1], 0.0)
            step(V.scalar_tensor_tensor(apad[:, :, TAPS - 1:], tanhg[:], 1.0, val[:], ALU.add, ALU.mult))

        def conv_tap(k):
            sync()
            for j in range(QD):
                src = apad[:, j, k:k + S]
                w = cw[:, k * QD + j:k * QD + j + 1]
                if k == 0:
                    last = V.tensor_scalar(val[:, j, :], src, w, par[:, R_CB + j:R_CB + j + 1], ALU.mult, ALU.add)
                else:
                    last = V.scalar_tensor_tensor(val[:, j, :], src, w, val[:, j, :], ALU.mult, ALU.add)
            if k < TAPS - 1:
                step(last)
            else:
                last.then_inc(conv_ready, 1)

        def level_exponents(n):
            half = 1 << (n - 1)
            if n == 1:
                dve.wait_ge(bc_ready, 1)
            if n < 8:
                b = bc[:].rearrange("p (b two l) -> p b two l", two=2, l=half)
                e = ex[:].rearrange("p (b two l) -> p b two l", two=2, l=half)
                end = b[:, :, 0, half - 1:half].broadcast_to([P, 2 * S // (2 * half), half])
                V.tensor_tensor(e[:, :, 0, :], end, b[:, :, 0, :], ALU.subtract)
                if half < GLA_CHUNK:
                    last = V.tensor_tensor(e[:, :, 1, :], b[:, :, 1, :], end, ALU.subtract)
                else:
                    last = V.tensor_copy(e[:, :, 1, :], b[:, :, 1, :])
                last.then_inc(exps_wanted, 1)
                return
            b = bc[:].rearrange("p (h c l) -> p h c l", h=2, l=GLA_CHUNK)
            e = ex[:].rearrange("p (h c l) -> p h c l", h=2, l=GLA_CHUNK)

            V.tensor_tensor(e[:, :, 1, :], b[:, :, 1, GLA_CHUNK - 1:GLA_CHUNK].broadcast_to([P, 2, GLA_CHUNK]), b[:, :, 1, :], ALU.subtract)
            V.tensor_tensor(e[:, :, 0, :], b[:, :, 0, GLA_CHUNK - 1:GLA_CHUNK].broadcast_to([P, 2, GLA_CHUNK]), b[:, :, 0, :], ALU.subtract)
            V.tensor_copy(e[:, :, 2, :], b[:, :, 2, :])
            step(V.tensor_tensor(e[:, :, 3, :], b[:, :, 3, :], b[:, :, 2, GLA_CHUNK - 1:GLA_CHUNK].broadcast_to([P, 2, GLA_CHUNK]), ALU.add))
            sync()
            V.tensor_tensor(e[:, :, 0, :], e[:, :, 0, :], b[:, :, 1, GLA_CHUNK - 1:GLA_CHUNK].broadcast_to([P, 2, GLA_CHUNK]), ALU.add).then_inc(exps_wanted, 1)

        def level_scale(n):
            dve.wait_ge(exps_ready, n)
            dve.wait_ge(level_sums, n)
            V.tensor_tensor(lqk[:, 0:2 * S], gqk[:, 0:2 * S], ex[:], ALU.mult)
            V.tensor_tensor(lqk[:, 2 * S:4 * S], gqk[:, 2 * S:4 * S], ex[:], ALU.mult).then_inc(level_ready, 1)

        def level_add(n):
            dve.wait_ge(level_sums, n + 1)
            if n == 8:
                V.tensor_copy(att[:, :, 1, :].rearrange("p (b h) t -> p b h t", b=2),
                              fb[:, :, 0:2 * P].rearrange("p b (h t) -> p b h t", h=2)).then_inc(att_ready, 1)
                return
            src = fb[:].rearrange("p b (h t n) -> p (b h) t n", h=2, t=TT)
            dst = att[:, :, 0:3:2, :]
            mask = (ident[:] if n == 0 else masks[:, n - 1, :]).unsqueeze(1).unsqueeze(1).broadcast_to([P, 4, TT, P])
            if n == 0:
                step(V.tensor_tensor(dst, src, mask, ALU.mult))
                return
            t = tmpg[:].rearrange("p (h t n) -> p h t n", h=4, t=TT)
            if n == 1:
                dve.wait_ge(consts, 2)
            step(V.tensor_tensor(t, src, mask, ALU.mult))
            sync()
            step(V.tensor_tensor(dst, dst, t, ALU.add))

        gb0 = FIRST["gB", 0]
        norm_at = {}
        for k, name_ in enumerate(("mq", "mk", "mq2", "mk2")):
            norm_at[LAST[name_, 0] + 10] = (k, "ms")
            norm_at[LAST[name_, 0] + 12] = (k, "scale")
        for c in range(4, UP1 + 12):
            split(c)
            if c == 14:
                dve.wait_ge(par_turned, 1)
                flat0 = fb[:].rearrange("p b n -> p (b n)")
                V.tensor_copy(par[:, KD:R_ALL], flat0[:, KD:R_ALL])
                V.tensor_scalar(parh[:], flat0[:, 0:R_ALL], 0.5, None, ALU.mult)
                V.tensor_copy(cw[:], flat0[:, P:P + TAPS * QD])
                fsrc = flat0[:, 2 * P:5 * P].rearrange("p (w n) -> p w n", w=FFN_TAPS)
                V.tensor_scalar(fw[:, :, 0:FT], fsrc[:, :, 0:FT], 0.5, None, ALU.mult)
                V.tensor_copy(fw[:, :, FT:2 * FT], fsrc[:, :, FT:2 * FT]).then_inc(par_ready, 1)
            if c == 20:
                dve.wait_ge(par_ready, 1)
                earlier()
                glu()
            if 21 <= c < 21 + TAPS:
                earlier()
                conv_tap(c - 21)
            if c == 32:
                earlier()
                dve.wait_ge(la_sums, 1)
                z = fb[:, :, 0:S]
                m, n_ = ex[:].rearrange("p (t n) -> p t n", t=TT), lqk[:, 0:2 * S].rearrange("p (t n) -> p t n", t=TT)
                V.tensor_scalar(m, z, 0.0, None, ALU.min)
                step(V.tensor_scalar(n_, z, 0.0, None, ALU.max))
                sync()
                V.tensor_tensor(lqk[:, 0:2 * S], lqk[:, 0:2 * S], ex[:], ALU.subtract).then_inc(la_abs, 1)
            if c == 34:
                earlier()
                dve.wait_ge(la_exp, 1)
                V.tensor_tensor(ex[:], ex[:], lqk[:, 0:2 * S], ALU.subtract).then_inc(la_ready, 1)
            if c == 46:
                earlier()
                wait_taken(dve, NUMBER["gr", 0])
                step(V.scalar_tensor_tensor(gr[:].rearrange("p j s -> p (j s)"), tmpg[:], 1.0,
                                            gr[:].rearrange("p j s -> p (j s)"), ALU.add, ALU.mult))
            if c == 56:
                earlier()
                dve.wait_ge(mean_sums, 1)
                V.scalar_tensor_tensor(val[:], quad(fb[:, 0, 0:S]), -1.0 / CONV_CH, val[:], ALU.mult, ALU.add).then_inc(xc_ready, 1)
            if c in norm_at:
                k, what = norm_at[c]
                earlier()
                if what == "ms":
                    dve.wait_ge(norm_sums, k + 1)
                    V.tensor_scalar(ms[:], fa[:, 0, 0:8], 1.0 / HD, EPS, ALU.mult, ALU.add).then_inc(ms_ready, 1)
                elif k % 2 == 0:
                    dve.wait_ge(rs_ready, (2, 5)[k // 2])
                    V.tensor_scalar(rq[:, k // 2, :], ms[:], HD ** -0.5, None, ALU.mult).then_inc(qk_normed, 1)
                else:
                    dve.wait_ge(rs_spread, (3, 4)[k // 2])
                    dst = mk[:, 4 * (k // 2):4 * (k // 2) + 4, :]
                    V.tensor_tensor(dst, dst, fa[:].rearrange("p b (j s) -> p (b j) s", j=2), ALU.mult).then_inc(qk_normed, 1)
            if c == 62:
                earlier()
                dve.wait_ge(var_sums, 1)
                V.tensor_scalar(ms[:, 0:TT], fb[:, 1, 0:TT], 1.0 / CONV_CH, EPS, ALU.mult, ALU.add).then_inc(ms_ready, 1)
            if c == 64:
                earlier()
                dve.wait_ge(rs_spread, 2)
                dve.wait_ge(xc_ready, 1)
                step(V.tensor_tensor(val[:], val[:], quad(fb[:, 1, 0:S]), ALU.mult))
                sync()
                for j in range(QD):
                    last = V.tensor_scalar(val[:, j, :], val[:, j, :], parh[:, R_LG + j:R_LG + j + 1],
                                           parh[:, R_LB + j:R_LB + j + 1], ALU.mult, ALU.add)
                last.then_inc(yh_ready, 1)
            if c == 68:
                earlier()
                dve.wait_ge(ytanh_ready, 1)
                V.scalar_tensor_tensor(full[:, U_A % 2, :, :], tanhg[:], 1.0, val[:], ALU.add, ALU.mult).then_inc(unit_full, 1)
            if c == 70:
                earlier()
                unit(U_A)
            if c == 71:
                earlier()
                level_add(0)
            for n in range(1, 9):
                if c == 72 + 4 * n:
                    earlier()
                    level_exponents(n)
                if c == 73 + 4 * n:
                    earlier()
                    level_scale(n)
                if c == 75 + 4 * n:
                    earlier()
                    level_add(n)
            if c == 113:
                earlier()
                dve.wait_ge(gla_o, 1)
                dve.wait_ge(gla_osq, 1)
                V.scalar_tensor_tensor(gr[:].rearrange("p j s -> p (j s)"), fa[:].rearrange("p b n -> p (b n)"),
                                       par[:, R_GLA:R_GLA + 1], gr[:].rearrange("p j s -> p (j s)"),
                                       ALU.mult, ALU.mult).then_inc(gla_r, 1)
            if c == 117:
                earlier()
                dve.wait_ge(gla_oss, 1)
                V.tensor_scalar(ms[:], fb[:, 0, 0:8], 1.0 / GLA_DV, EPS, ALU.mult, ALU.add).then_inc(ms_ready, 1)
            if c == 119:
                earlier()
                dve.wait_ge(rs_spread, 5)
                dve.wait_ge(gla_r, 1)
                V.tensor_tensor(full[:, U_B % 2, :, :], gr[:], fb[:].rearrange("p b (j s) -> p (b j) s", j=2), ALU.mult).then_inc(unit_full, 1)
            if c == 121:
                earlier()
                unit(U_B)
            i = c - gb0
            if 0 <= i < 38:
                earlier()
                if i % 4 == 3 and i // 4 < HEADS:
                    h = i // 4
                    s_ = sc[:, h % 2, :]
                    b = 2 + 6 * (h % 2)
                    dve.wait_ge(sc_sums, h + 1)
                    if h == 0:
                        dve.wait_ge(chunk_used, gb0)
                    step(V.tensor_tensor(s_, fa[:, h % 2, 0:3 * P], cmask[:].rearrange("p a b -> p (a b)"), ALU.add))
                    sync()
                    V.tensor_reduce(small[:, b:b + 1], s_[:, 0:P], AX_X, ALU.max)
                    step(V.tensor_reduce(small[:, b + 1:b + 2], s_[:, P:3 * P], AX_X, ALU.max))
                    sync()
                    V.scalar_tensor_tensor(small[:, b:b + 2], small[:, b:b + 2], -1.0,
                                           rq[:, h // 4, 2 * (h % 4):2 * (h % 4) + 2], ALU.mult, ALU.mult).then_inc(sc_ready, 1)
                if i % 4 == 0 and 4 <= i < 36:
                    h = i // 4 - 1
                    b = 4 + 6 * (h % 2)
                    dve.wait_ge(sc_exp, h + 1)
                    step(V.reciprocal(small[:, b:b + 2], small[:, b:b + 2]))
                    sync()
                    V.tensor_scalar(sc[:, h % 2, 0:P], sc[:, h % 2, 0:P], small[:, b:b + 1], None, ALU.mult)
                    V.tensor_scalar(sc[:, h % 2, P:3 * P], sc[:, h % 2, P:3 * P], small[:, b + 1:b + 2], None, ALU.mult).then_inc(pr_ready, 1)
                if i % 4 == 0 and i >= 8:
                    h = i // 4 - 2
                    dve.wait_ge(pv_sums, h + 1)
                    V.tensor_copy(full[:, (U_C + h) % 2, 0, :], fb[:, 1, 0:S]).then_inc(unit_full, 1)
                if i % 4 == 1 and i >= 9:
                    unit(U_C + (i - 9) // 4)
            for b in range(3):
                for g in range(4):
                    name = "g" + "ABC"[b]
                    q = slice(4 * g, 4 * g + 4)
                    if c == LAST[name, g] + (6 if b < 2 else 5):
                        earlier()
                        wait_taken(dve, NUMBER[name, g])
                        if b == 0:
                            wait_taken(dve, NUMBER["yA", g])
                            V.scalar_tensor_tensor(merged[:, q, :], gt[:], 1.0, merged[:, q, :], ALU.add, ALU.mult).then_inc(gate_merged, 1)
                        else:
                            wait_taken(dve, NUMBER["yB" if b == 1 else "yC", g])
                            step(V.scalar_tensor_tensor(yb[:, q, :], gt[:], 1.0, yb[:, q, :], ALU.add, ALU.mult))
                            sync()
                            if b == 1:
                                V.tensor_tensor(merged[:, q, :], merged[:, q, :], yb[:, q, :], ALU.add).then_inc(gate_merged, 1)
                            else:
                                V.tensor_tensor(full[:, (U_M + g) % 2, :, :], merged[:, q, :], yb[:, q, :], ALU.add).then_inc(unit_full, 1)
                    if b == 2 and c == LAST[name, g] + 6:
                        earlier()
                        unit(U_M + g)
            if c == FIRST["gC", 0] + 8:
                earlier()
                dve.wait_ge(p_turned, 1)
                V.tensor_copy(full[:, U_P % 2, 0:2, :].rearrange("p j s -> p (j s)"), fa[:, 0, :]).then_inc(unit_full, 1)
            if c == FIRST["gC", 0] + 10:
                earlier()
                unit(U_P)
            for g in range(4):
                if c == LAST["wout", g] + 4:
                    earlier()
                    number = NUMBER["wout", g]
                    q = slice(4 * g, 4 * g + 4)
                    dve.wait_ge(chunk_used, LAST["wout", g] + 1)
                    V.tensor_tensor(xT[:, q, :], xT[:, q, :], acc[number % 2][:], ALU.add).then_inc(taken[number % 2], 1)
                    wait_taken(dve, number)
                    if g == 0:
                        step(V.memset(sqsum[:], 0.0))
                    for j in range(QD):
                        last = V.tensor_scalar(full[:, (U_X1 + g) % 2, j, :], xT[:, 4 * g + j, :],
                                               par[:, R_FFN + 4 * g + j:R_FFN + 4 * g + j + 1], None, ALU.mult)
                        if j == 0:
                            last.then_inc(x_new, 1)
                    last.then_inc(unit_full, 1)
                if c == LAST["wout", g] + 5:
                    earlier()
                    unit(U_X1 + g)
                if c == LAST["wout", g] + 6:
                    earlier()
                    dve.wait_ge(xsq_ready, g + 1)
                    if g == 0:
                        sync()
                    else:
                        dve.wait_ge(xsum_ready, g)
                    V.tensor_tensor(sqsum[:], sqsum[:], sqx[:], ALU.add).then_inc(xsum_ready, 1)
            if c == UP1 + 2:
                earlier()
                dve.wait_ge(xss, 1)
                V.tensor_scalar(ms[:, 0:TT], fa[:, 0, 0:TT], 1.0 / D, EPS, ALU.mult, ALU.add).then_inc(ms_ready, 1)
            if c == UP1 + 3:
                earlier()
                dve.wait_ge(rs_spread, 6)
                step(V.tensor_copy(rB[:], fa[:, 0, 0:S]))
                V.memset(upg[:, :, 0:2], 0.0)
                step(V.memset(upv[:, :, 0:2], 0.0))
                sync()

        d0 = steps[0]

        def up(c0, pairs, group0, pair0, u0, d0):
            with dve.Fori(0, pairs) as i:
                def conv(src, dst, col, taps, done):
                    dve.wait_ge(tap_ready, i * 2 + taps)
                    for j in range(QD):
                        last = V.scalar_tensor_tensor(dst[:, j, :], src[:, j, 1:1 + S], fw[:, 1, bass.ds(i * QD + (col + j), 1)],
                                                      dst[:, j, :], ALU.mult, ALU.add)
                    last.then_inc(dve_step, 1)

                def conv2(src, dst, col, count, done):
                    dve.wait_ge(dve_step, i * 2 + count)
                    for j in range(QD):
                        last = V.scalar_tensor_tensor(dst[:, j, :], src[:, j, 0:S], fw[:, 0, bass.ds(i * QD + (col + j), 1)],
                                                      dst[:, j, :], ALU.mult, ALU.add)
                    last.then_inc(done, 1)

                dve.wait_ge(chunk_split, i * 16 + (c0 + 12))
                dve.wait_ge(chunk_used, i * 16 + (c0 + 8))
                V.tensor_tensor(upg[:, :, 2:], acc[0][:], quad(rB[:]), ALU.mult).then_inc(taken[0], 1)
                split(c0 + 12, i, 16)
                conv(upg, cg, 4 * pair0, 2 * pair0 + 1, None)
                split(c0 + 13, i, 16)
                conv2(upg, cg, 4 * pair0, d0 + 1, cg_ready)
                split(c0 + 14, i, 16)
                split(c0 + 15, i, 16)
                dve.wait_ge(tg_ready, i + (pair0 + 1))
                dve.wait_ge(cg_ready, i + (pair0 + 1))
                V.scalar_tensor_tensor(cg[:], tg[:], 1.0, cg[:], ALU.add, ALU.mult)
                for k in range(16, 20):
                    split(c0 + k, i, 16)
                earlier()
                dve.wait_ge(chunk_used, i * 16 + (c0 + 16))
                V.tensor_tensor(upv[:, :, 2:], acc[1][:], quad(rB[:]), ALU.mult).then_inc(taken[1], 1)
                split(c0 + 20, i, 16)
                conv(upv, cv, FT + 4 * pair0, 2 * pair0 + 2, None)
                split(c0 + 21, i, 16)
                conv2(upv, cv, FT + 4 * pair0, d0 + 2, cv_ready)
                split(c0 + 22, i, 16)
                earlier()
                dve.wait_ge(cv_ready, i + (pair0 + 1))
                V.tensor_tensor(full[:, 0, :, :], cg[:], cv[:], ALU.mult).then_inc(unit_full, 1)
                split(c0 + 23, i, 16)
                earlier()
                dve.wait_ge(unit_high, i + (u0 + 1))
                V.tensor_tensor(f_lo[:, bass.ds(i * QD, QD), :], full[:, 0, :, :], f_hi[:, bass.ds(i * QD, QD), :].bitcast(F32),
                                ALU.subtract).then_inc(unit_split, 1)
                for k in range(24, 28):
                    split(c0 + k, i, 16)
            return d0 + 2 * pairs

        d0 = up(UP1, PAIRS1, NG_UP1, 0, U_F, d0)
        n = K1 // 2
        with dve.Fori(0, 2) as i:
            for k in range(12, 12 + 2 * n):
                split(DOWN1 + k, i, 2 * n)
                for half in range(2):
                    if k == half * n + n + 3:
                        earlier()
                        dve.wait_ge(chunk_used, i * (2 * n) + (DOWN1 + half * n + n))
                        v = xT[:, bass.ds(i * 8 + 4 * half, 4), :]
                        V.tensor_tensor(v, v, acc[half][:], ALU.add).then_inc(taken[half], 1)
        d0 = up(UP2, PAIRS2, NG_UP2, PAIRS1, U_F + PAIRS1, d0)
        dve.wait_ge(xsum_ready, 4)
        earlier()
        V.memset(sqsum[:], 0.0).then_inc(dve_step, 1)
        d0 += 1
        dve.wait_ge(dve_step, d0)
        n = K2 // 2
        with dve.Fori(0, 2) as i:
            for k in range(12, 12 + 2 * n):
                split(DOWN2 + k, i, 2 * n)
                for half in range(2):
                    if k == half * n + n + 3:
                        earlier()
                        dve.wait_ge(chunk_used, i * (2 * n) + (DOWN2 + half * n + n))
                        v = xT[:, bass.ds(i * 8 + 4 * half, 4), :]
                        V.tensor_tensor(v, v, acc[half][:], ALU.add).then_inc(taken[half], 1)
                        dve.wait_ge(taken[half], i + (NG_DOWN2 // 2 + 1))
                        for j in range(QD):
                            last = V.tensor_scalar(full[:, half, j, :], xT[:, bass.ds(i * 8 + 4 * half + j, 1), :],
                                                   par[:, bass.ds(i * 8 + (R_PLE + 4 * half + j), 1)], None, ALU.mult)
                            if j == 0:
                                last.then_inc(x_new, 1)
                        last.then_inc(unit_full, 1)
                    if k == half * n + n + 4:
                        earlier()
                        dve.wait_ge(unit_high, i * 2 + (U_X2 + half + 1))
                        q = bass.ds(i * 8 + 4 * half, 4)
                        V.tensor_tensor(h_lo[:, q, :], full[:, half, :, :], h_hi[:, q, :].bitcast(F32), ALU.subtract).then_inc(unit_split, 1)
                    if k == half * n + n + 5:
                        earlier()
                        dve.wait_ge(xsq_ready, i * 2 + (4 + half + 1))
                        dve.wait_ge(xsum_ready, i * 2 + (4 + half))
                        V.tensor_tensor(sqsum[:], sqsum[:], sqx[:], ALU.add).then_inc(xsum_ready, 1)
        for c in range(PLEG + 12, END + 5):
            if c < END:
                split(c)
            if PLEG + 12 <= c:
                earlier()
            if c == PLEG + 12:
                dve.wait_ge(xss, 2)
                V.tensor_scalar(ms[:, 0:TT], fa[:, 0, 0:TT], 1.0 / D, EPS, ALU.mult, ALU.add).then_inc(ms_ready, 1)
                dve.wait_ge(rs_ready, 9)
                V.tensor_scalar(small[:, 14:15], ms[:, 0:1], 0.5, None, ALU.mult)
                V.tensor_scalar(small[:, 13:14], ms[:, 1:2], 0.5, None, ALU.mult).then_inc(r2_ready, 1)
            for g in range(4):
                if c == PLEG + 8 * g + (14 if g == 0 else 12):
                    number = NG_PLEG + g
                    cols = slice(g * W, (g + 1) * W)
                    wait_taken(dve, number)
                    dve.wait_ge(x2_taken, g + 1)
                    if g >= 2:
                        dve.wait_ge(out_landed[g % 2], 16 * TT)
                    V.scalar_tensor_tensor(fin[:, g % 2, :, :], gt2[:], 1.0, ple[:, :, cols], ALU.add, ALU.mult).then_inc(pg_ready, 1)
                    dve.wait_ge(pg_ready, g + 1)
                    V.tensor_tensor(fin[:, g % 2, :, :], fin[:, g % 2, :, :], x2tok[:, :, cols], ALU.add).then_inc(out_ready, 1)

    block.__exit__(None, None, None)


_INS = ["x", "p", "norm_mix_g", "w_in", "conv_w", "conv_b", "conv_ln_g", "conv_ln_b", "w_conv_out",
        "gla_w_a2", "gla_b_a", "gla_norm_g", "w_gla_out", "moba_q_norm_g", "moba_k_norm_g", "w_moba_out",
        "w_gate", "b_gate", "w_out", "norm_ffn_g", "w_up", "ffn_conv_w", "w_down",
        "norm_ple_g", "w_ple_gate", "w_ple"]


def kernel(**inputs):
    import concourse.bacc as bacc
    from concourse.bass_utils import run_bass_kernel_spmd

    nc = bacc.Bacc("TRN2", target_bir_lowering=False, num_devices=1)
    arrays, args = {}, []
    for name in _INS:
        a = np.ascontiguousarray(inputs[name])
        arrays[f"in_{name}"] = a
        args.append(nc.dram_tensor(f"in_{name}", a.shape, mybir.dt.from_np(a.dtype), kind="ExternalInput").ap())
    out = nc.dram_tensor("out_0", (1, S, D), F32, kind="ExternalOutput").ap()
    trunk(nc, *args, out)
    r = run_bass_kernel_spmd(nc, [arrays], core_ids=[0])
    return r.results[0]["out_0"]
```

```python
import numpy as np

import concourse.bass as bass
from concourse import mybir

F32 = mybir.dt.float32
F32R = mybir.dt.float32r
ALU = mybir.AluOpType
ACT = mybir.ActivationFunctionType
AX_X = mybir.AxisListType.X

P = 128
D = 2048
S = 256
TT = S // P
KD = D // P
EPS = 1e-6
CONV_CH = D // 4
TAPS = 31
GLA_HEADS, GLA_DK, GLA_DV, GLA_RANK, GLA_TAU, GLA_CHUNK = 4, 64, 128, 16, 16.0, 64
HEADS, HD = 8, 128
PLE = 256
FFN = 5632
FT = FFN // P
FFN_TAPS = 3

RING = 4
W = 512
CH = 1024
QD = 4

C_VAL, C_GATE, C_QK, C_GV, C_GR, C_GA, C_MQ, C_MK, C_MV = 0, 512, 1024, 1536, 2048, 2560, 2576, 3600, 4624

GROUPS = []


def _plan():
    c = 0
    for name, count, chunks in (("val", 1, 8), ("gate", 1, 8), ("qk", 1, 8), ("alow", 1, 2),
                                ("gv", 1, 8), ("gr", 1, 8), ("mq", 1, 8), ("mk", 1, 8),
                                ("mq2", 1, 8), ("mk2", 1, 8), ("mv", 2, 8), ("yA", 4, 2),
                                ("gA", 4, 8), ("yB", 4, 2), ("gB", 4, 8), ("yC", 4, 4),
                                ("gC", 4, 8), ("wout", 4, 8), ("ple", 4, 1)):
        for g in range(count):
            GROUPS.append((name, g, c, chunks))
            c += chunks
    return c


UP1 = _plan()
PAIRS1, PAIRS2 = 6, 5
K1, K2 = PAIRS1 * QD, PAIRS2 * QD
DOWN1 = UP1 + 16 * PAIRS1
UP2 = DOWN1 + 4 * K1 // 2
DOWN2 = UP2 + 16 * PAIRS2
PLEG = DOWN2 + 4 * K2 // 2
END = PLEG + 32
GROUP_AT = {}
for _n, (_name, _g, _c0, _k) in enumerate(GROUPS):
    for _j in range(_k):
        GROUP_AT[_c0 + _j] = (_name, _g, _j, _k, _n)
FIRST = {(name, g): c0 for name, g, c0, _ in GROUPS}
LAST = {(name, g): c0 + k - 1 for name, g, c0, k in GROUPS}
NUMBER = {(name, g): n for n, (name, g, _, _) in enumerate(GROUPS)}
N_STRAIGHT = len(GROUPS)
PAR = 10
GLU = 20
DECAY = 28
SILU_R = LAST["gr", 0] + 5
CONV_LN = 56
GLA = 70
MOBA = FIRST["yB", 0]

U_H = 0
U_A = U_H + 8
U_B = U_A + 1
U_C = U_B + 1
U_P = U_C + HEADS
U_M = U_P + 1
U_X1 = U_M + 4
U_F = U_X1 + 4
U_X2 = U_F + PAIRS1 + PAIRS2

R_MIX, R_CB, R_LG, R_LB, R_GLA, R_Q, R_K, R_BG, R_FFN, R_PLE, R_ALL = 0, 16, 20, 24, 28, 29, 30, 31, 79, 95, 111

START = 8

STAT_CONV = 8

MASKED = -1e30


def trunk(nc, x, p, norm_mix_g, w_in, conv_w, conv_b, conv_ln_g, conv_ln_b, w_conv_out,
          gla_w_a2, gla_b_a, gla_norm_g, w_gla_out, moba_q_norm_g, moba_k_norm_g, w_moba_out,
          w_gate, b_gate, w_out, norm_ffn_g, w_up, ffn_conv_w, w_down,
          norm_ple_g, w_ple_gate, w_ple, out):
    base = (nc.sbuf_base + 31) // 32 * 32
    KB = 1024
    top = [base]

    def at(name, shape, dtype, offset):
        return nc.alloc_sbuf_tensor_at(name, shape, dtype, offset=offset)

    def new(name, shape, dtype=F32):
        n = 4 * int(np.prod(shape[1:]))
        t = at(name, shape, dtype, top[0])
        top[0] += (n + 31) // 32 * 32
        return t

    raw = new("raw", [P, RING, CH])
    w_hi = new("w_hi", [P, RING, CH], F32R)
    w_lo = new("w_lo", [P, RING, CH], F32R)
    h_hi = new("h_hi", [P, KD, S], F32R)
    h_lo = new("h_lo", [P, KD, S], F32R)
    xT = new("xT", [P, KD, S])
    full = new("full", [P, 2, QD, S])
    ms = new("ms", [P, 10])
    par = new("par", [P, R_ALL])
    parh = new("parh", [P, R_ALL])
    cw = new("cw", [P, TAPS * QD])
    fw = new("fw", [P, FFN_TAPS, 2 * FT])
    ident = new("ident", [P, P])
    ones = new("ones", [P, P])
    tri = new("tri", [P, P])
    cmask = new("cmask", [P, 3, P])
    rq = new("rq", [P, 2, 8])
    rB = new("rB", [P, S])
    small = new("small", [P, 16])
    arena = top[0]
    assert arena + 90 * KB <= nc.sbuf_usable_end, (arena, nc.sbuf_usable_end)

    def ar(name, shape, kb, dtype=F32):
        return at(name, shape, dtype, arena + int(kb * KB))

    xtok = ar("xtok", [P, TT, D], 0)
    junk = ar("junk", [P, 4 * TT, W], 48)
    pst = ar("pst", [P, 6, P], 32)
    val = ar("val", [P, QD, S], 0)
    tanhg = ar("tanhg", [P, QD, S], 4)
    vsum = ar("vsum", [P, S], 13)
    apad = ar("apad", [P, QD, TAPS - 1 + S], 8)
    a_hi = ar("a_hi", [P, QD, S], 16, F32R)
    a_lo = ar("a_lo", [P, QD, S], 20, F32R)
    sqm = ar("sqm", [P, QD, S], 24)
    masks = ar("masks", [P, 7, P // 2], 28)
    merged = ar("merged", [P, KD, S], 0)
    yb = ar("yb", [P, KD, S], 16)
    mq = ar("mq", [P, HEADS, S], 32)
    mk = ar("mk", [P, HEADS, S], 40)
    mv = ar("mv", [P, TT, HEADS * HD], 48)
    gqk = ar("gqk", [P, 4 * S], 56)
    gv = ar("gv", [P, TT, W], 60)
    gr = ar("gr", [P, QD, S], 64)
    bc = ar("bc", [P, 2 * S], 68)
    ex = ar("ex", [P, 2 * S], 70)
    lqk = ar("lqk", [P, 4 * S], 72)
    alow = ar("alow", [GLA_RANK, S], 72)
    wa2 = ar("wa2", [GLA_RANK, S], 73)
    brow = ar("brow", [1, S], 74)
    att = ar("att", [P, 3 * GLA_HEADS, P], 76)
    tmpg = ar("tmpg", [P, QD * S], 82)
    gt = ar("gt", [P, QD, S], 86)
    o_hi = ar("o_hi", [P, QD, S], 68, F32R)
    o_lo = ar("o_lo", [P, QD, S], 72, F32R)
    c_hi = ar("c_hi", [P, HEADS, S], 56, F32R)
    c_lo = ar("c_lo", [P, HEADS, S], 64, F32R)
    sc = ar("sc", [P, 2, 3 * P], 82)
    pT = ar("pT", [P, 2, 3 * P], 78)
    m_hi = ar("m_hi", [P, KD, S], 32, F32R)
    m_lo = ar("m_lo", [P, KD, S], 48, F32R)
    p_hi = ar("p_hi", [P, 2, S], 64, F32R)
    p_lo = ar("p_lo", [P, 2, S], 66, F32R)
    ptok = ar("ptok", [P, TT, PLE], 76)
    sqx = ar("sqx", [P, QD, S], 0)
    sqfold = ar("sqfold", [P, S], 4)
    sqsum = ar("sqsum", [P, S], 5)
    upg = ar("upg", [P, QD, 2 + S], 0)
    upv = ar("upv", [P, QD, 2 + S], 4.25)
    cg = ar("cg", [P, QD, S], 8.5)
    cv = ar("cv", [P, QD, S], 12.5)
    tg = ar("tg", [P, QD, S], 16.5)
    f_hi = ar("f_hi", [P, K1, S], 20.5, F32R)
    f_lo = ar("f_lo", [P, K1, S], 44.5, F32R)
    ple = ar("ple", [P, TT, D], 68.5)
    x2tok = ar("x2tok", [P, TT, D], 20.5)
    gt2 = ar("gt2", [P, TT, W], 8.5)
    fin = ar("fin", [P, 2, TT, W], 36.5)

    acc = [nc.alloc_psum_tensor(f"acc{i}", [P, QD, S], F32) for i in range(2)]
    fa = nc.alloc_psum_tensor("fa", [P, 2, 512], F32)
    fb = nc.alloc_psum_tensor("fb", [P, 2, 512], F32)

    def flat(t):
        return t[:].rearrange("p a b -> p (a b)")

    def sem(name):
        return nc.alloc_semaphore(name)

    chunk_landed = [sem(f"chunk_landed{i}") for i in range(RING)]
    chunk_high, chunk_split, chunk_used = sem("chunk_high"), sem("chunk_split"), sem("chunk_used")
    taken = [sem("taken0"), sem("taken1")]
    unit_full, unit_high, unit_split = sem("unit_full"), sem("unit_high"), sem("unit_split")
    x_landed = [sem(f"x_landed{q}") for q in range(4)]
    gain_landed, par_landed, p_landed = sem("gain_landed"), sem("par_landed"), sem("p_landed")
    out_landed = [sem("out_landed0"), sem("out_landed1")]
    consts = sem("consts")
    ms_ready, rs_ready = sem("ms_ready"), sem("rs_ready")
    gain_turned, gain_ready, par_turned, par_ready = (
        sem(n) for n in ("gain_turned", "gain_ready", "par_turned", "par_ready"))
    ssq_ready = sem("ssq_ready")
    xq_turned = sem("xq_turned")
    xq_taken, xq_taken_act = sem("xq_taken"), sem("xq_taken_act")
    rs_spread, rb_ready = sem("rs_spread"), sem("rb_ready")
    act_step, dve_step, pool_step = sem("act_step"), sem("dve_step"), sem("pool_step")
    la_sums, la_abs, la_exp, la_ready = sem("la_sums"), sem("la_abs"), sem("la_exp"), sem("la_ready")
    bc_sums, bc_ready = sem("bc_sums"), sem("bc_ready")
    conv_ready, mean_sums, xc_ready, xcsq_ready, var_sums, yh_ready, ytanh_ready = (
        sem(n) for n in ("conv_ready", "mean_sums", "xc_ready", "xcsq_ready", "var_sums", "yh_ready", "ytanh_ready"))
    xcsq_folded = sem("xcsq_folded")
    norm_sums, qk_normed = sem("norm_sums"), sem("qk_normed")
    exps_wanted, exps_ready, level_ready, level_sums, att_ready = (
        sem(n) for n in ("exps_wanted", "exps_ready", "level_ready", "level_sums", "att_ready"))
    gla_o, gla_osq, gla_oss, gla_r = sem("gla_o"), sem("gla_osq"), sem("gla_oss"), sem("gla_r")
    sc_sums, sc_ready, sc_exp, pr_ready, pr_turned, pT_ready, pv_sums = (
        sem(n) for n in ("sc_sums", "sc_ready", "sc_exp", "pr_ready", "pr_turned", "pT_ready", "pv_sums"))
    gate_ready, gate_merged = sem("gate_ready"), sem("gate_merged")
    p_turned = sem("p_turned")
    x_new, xsq_ready, xsum_ready, xss = sem("x_new"), sem("xsq_ready"), sem("xsum_ready"), sem("xss")
    tap_ready, cg_ready, tg_ready = sem("tap_ready"), sem("cg_ready"), sem("tg_ready")
    x2_turned, x2_taken = sem("x2_turned"), sem("x2_taken")
    r2_ready, pg_ready, out_ready = sem("r2_ready"), sem("pg_ready"), sem("out_ready")
    tile0_sums, tile_gate = sem("tile0_sums"), sem("tile_gate")
    cv_ready, folded = sem("cv_ready"), sem("folded")

    def unit_dst(u):
        if u < U_A:
            return h_hi[:, 2 * u:2 * u + 2, :], h_lo[:, 2 * u:2 * u + 2, :], 2
        if u == U_A:
            return a_hi[:], a_lo[:], 4
        if u == U_B:
            return o_hi[:], o_lo[:], 4
        if u < U_P:
            return c_hi[:, u - U_C:u - U_C + 1, :], c_lo[:, u - U_C:u - U_C + 1, :], 1
        if u == U_P:
            return p_hi[:], p_lo[:], 2
        if u < U_X1:
            k = 4 * (u - U_M)
            return m_hi[:, k:k + 4, :], m_lo[:, k:k + 4, :], 4
        k = 4 * (u - U_X1)
        return h_hi[:, k:k + 4, :], h_lo[:, k:k + 4, :], 4

    def wait_taken(eng, n):
        eng.wait_ge(taken[n % 2], n // 2 + 1)

    NG_UP1 = N_STRAIGHT
    NG_DOWN1 = NG_UP1 + 2 * PAIRS1
    NG_UP2 = NG_DOWN1 + 4
    NG_DOWN2 = NG_UP2 + 2 * PAIRS2
    NG_PLEG = NG_DOWN2 + 4
    assert NG_UP1 % 2 == 0

    rows = [(norm_mix_g[0], R_MIX), (conv_b[0], R_CB), (conv_ln_g[0], R_LG), (conv_ln_b[0], R_LB),
            (gla_norm_g[0], R_GLA), (moba_q_norm_g[0], R_Q), (moba_k_norm_g[0], R_K), (b_gate[0], R_BG),
            (norm_ffn_g[0], R_FFN), (norm_ple_g[0], R_PLE)]
    par_dmas = len(rows) + 1 + FFN_TAPS + 2

    block = nc.Block()
    block.__enter__()

    @block.sync
    def _(sp):
        def chunk(c, src, k, i=None, step=0):
            if i is not None:
                sp.wait_ge(chunk_split, i * step + (c - RING + 1))
            elif c >= RING:
                sp.wait_ge(chunk_split, c - RING + 1)
            sp.dma_start(raw[:, c % RING, :].rearrange("p (k n) -> p k n", k=k),
                         src.rearrange("(k p) n -> p k n", p=P)).then_inc(chunk_landed[c % RING], 16)

        for q in range(4):
            sp.dma_start(xtok[:, :, q * W:(q + 1) * W],
                         x[0, :, q * W:(q + 1) * W].rearrange("(t p) n -> p t n", p=P)).then_inc(x_landed[q], 16)
        wi, wg = w_in[0], w_gate[0]
        cols = {"val": C_VAL, "gate": C_GATE, "qk": C_QK, "gv": C_GV, "gr": C_GR, "mq": C_MQ,
                "mk": C_MK, "mq2": C_MQ + W, "mk2": C_MK + W}
        for name, g, c0, n in GROUPS:
            if name == "gB" and g == 1:
                sp.wait_ge(chunk_used, FIRST["gB", 0])
                sp.dma_start(ptok[:], p[0, 0].rearrange("(t p) n -> p t n", p=P)).then_inc(p_landed, 16)
            for j in range(n):
                c = c0 + j
                if name in cols:
                    chunk(c, wi[j * 256:(j + 1) * 256, cols[name]:cols[name] + W], 2)
                elif name == "alow":
                    chunk(c, wi[j * 1024:(j + 1) * 1024, C_GA:C_GA + P], 8)
                elif name == "mv":
                    chunk(c, wi[j * 256:(j + 1) * 256, C_MV + g * W:C_MV + (g + 1) * W], 2)
                elif name in ("gA", "gB", "gC"):
                    col = "ABC".index(name[1]) * D + g * W
                    chunk(c, wg[j * 256:(j + 1) * 256, col:col + W], 2)
                else:
                    w = {"yA": w_conv_out, "yB": w_gla_out, "yC": w_moba_out, "wout": w_out, "ple": w_ple}[name][0]
                    chunk(c, w[j * 256:(j + 1) * 256, g * W:(g + 1) * W], 2)

        def up(c0, pairs, pair0):
            with sp.Fori(0, pairs) as i:
                for part in range(2):
                    for j in range(8):
                        chunk(c0 + 8 * part + j,
                              w_up[0][j * 256:(j + 1) * 256, bass.ds(i * W + (part * FFN + pair0 * W), W)],
                              2, i, 16)

        def down(c0, kt, kt0):
            n = kt // 2
            with sp.Fori(0, 2) as i:
                for half in range(2):
                    for j in range(n):
                        chunk(c0 + half * n + j,
                              w_down[0][(kt0 + 2 * j) * P:(kt0 + 2 * j + 2) * P, bass.ds(i * 2 * W + half * W, W)],
                              2, i, 2 * n)

        up(UP1, PAIRS1, 0)
        down(DOWN1, K1, 0)
        up(UP2, PAIRS2, PAIRS1)
        down(DOWN2, K2, K1)
        with sp.Fori(0, 2) as i:
            for half in range(2):
                for j in range(8):
                    chunk(PLEG + 8 * half + j,
                          w_ple_gate[0][j * 256:(j + 1) * 256, bass.ds(i * 2 * W + half * W, W)], 2, i, 16)
        for g in range(4):
            for t in range(TT):
                if t == 0 or g == 3:
                    sp.wait_ge(out_ready, g + t + 1)
                sp.dma_start(out[0, t * P:(t + 1) * P, g * W:(g + 1) * W], fin[:, g % 2, t, :]).then_inc(out_landed[g % 2], 16)
        for s in range(2):
            sp.wait_ge(out_landed[s], 16 * 2 * TT)

    @block.gpsimd
    def _(pool):
        nc.gpsimd.memset(ones[:], 1.0).then_inc(pool_step, 1)
        nc.gpsimd.memset(small[:, 15:16], -0.5).then_inc(pool_step, 1)
        pool.wait_ge(pool_step, 2)
        nc.gpsimd.affine_select(out=ident[:], in_=ones[:], compare_op=ALU.is_equal, fill=0.0, base=0,
                                pattern=[[-1, P]], channel_multiplier=1).then_inc(consts, 1)
        def rsqrt(n, cols, at=0):
            pool.wait_ge(ms_ready, n)
            nc.gpsimd.tensor_tensor(ms[:, at:at + cols], ms[:, at:at + cols], small[:, 15:16].to_broadcast([P, cols]),
                                    ALU.pow).then_inc(rs_ready, 1)

        n = 2
        nc.gpsimd.memset(cmask[:], 0.0).then_inc(pool_step, 1)
        n += 1
        pool.wait_ge(pool_step, n)
        for b in (0, 2):
            nc.gpsimd.affine_select(out=cmask[:, b, :], in_=cmask[:, b, :], compare_op=ALU.is_ge, fill=MASKED,
                                    base=0, pattern=[[-1, P]], channel_multiplier=1).then_inc(pool_step, 1)
            n += 1
        rsqrt(1, TT)
        for v, r in rows:
            pool.dma_start(pst[r:r + v.shape[0] // P, 0, :], v.rearrange("(r p) -> r p", p=P)).then_inc(par_landed, 16)
        pool.dma_start(pst[0:TAPS * QD, 1, :], conv_w[0].rearrange("w (j p) -> (w j) p", p=P)).then_inc(par_landed, 16)
        for k in range(FFN_TAPS):
            pool.dma_start(pst[0:2 * FT, 2 + k, :], ffn_conv_w[0, k].rearrange("(r p) -> r p", p=P)).then_inc(par_landed, 16)
        pool.dma_start(wa2[:], gla_w_a2[0]).then_inc(par_landed, 16)
        pool.dma_start(brow[:], gla_b_a).then_inc(par_landed, 16)
        nc.gpsimd.memset(tri[:], 1.0 / GLA_TAU).then_inc(pool_step, 1)
        n += 1
        pool.wait_ge(pool_step, n)
        blocks = tri[:].rearrange("p (b n) -> p b n", n=GLA_CHUNK)
        nc.gpsimd.affine_select(out=blocks, in_=blocks, compare_op=ALU.is_ge, fill=0.0, base=0,
                                pattern=[[-GLA_CHUNK, P // GLA_CHUNK], [0, GLA_CHUNK]],
                                channel_multiplier=1).then_inc(pool_step, 1)
        n += 1
        pool.wait_ge(pool_step, n)
        nc.gpsimd.affine_select(out=tri[:], in_=tri[:], compare_op=ALU.is_ge, fill=0.0, base=0,
                                pattern=[[1, P]], channel_multiplier=-1).then_inc(pool_step, 1)
        n += 1
        nc.gpsimd.memset(masks[:], 1.0).then_inc(pool_step, 1)
        n += 1
        for i in range(7):
            half = 1 << i
            v = masks[:, i, :].rearrange("p (b l) -> p b l", l=half)
            pool.wait_ge(pool_step, n)
            nc.gpsimd.affine_select(out=v, in_=v, compare_op=ALU.is_ge, fill=0.0, base=0,
                                    pattern=[[-2 * half, P // (2 * half)], [0, half]],
                                    channel_multiplier=1).then_inc(pool_step, 1)
            n += 1
            pool.wait_ge(pool_step, n)
            nc.gpsimd.affine_select(out=v, in_=v, compare_op=ALU.is_ge, fill=0.0, base=half - 1,
                                    pattern=[[2 * half, P // (2 * half)], [0, half]],
                                    channel_multiplier=-1).then_inc(pool_step if i < 6 else consts, 1)
            n += 1
        for k, (cols, first) in enumerate(((8, 0), (TT, STAT_CONV), (8, 0), (8, 0), (8, 0), (8, 0), (TT, 0), (TT, 0))):
            rsqrt(2 + k, cols, first)

    @block.tensor
    def _(pe):
        def products(dst, stat_hi, stat_lo, mov_hi, mov_lo, first, last):
            nc.tensor.matmul(dst, stat_hi, mov_hi, start=first, stop=False, skip_group_check=True)
            nc.tensor.matmul(dst, stat_hi, mov_lo, start=False, stop=False, skip_group_check=True)
            return nc.tensor.matmul(dst, stat_lo, mov_hi, start=False, stop=last, skip_group_check=True)

        def feature_chunk(c, s, a_h, a_l, kt, first, last, i=None, step=0):
            pe.wait_ge(chunk_split, c + 1 if i is None else i * step + (c + 1))
            for k in range(2):
                for j in range(QD):
                    w = slice(k * W + j * P, k * W + (j + 1) * P)
                    mm = products(acc[s][:, j, :], w_hi[:, c % RING, w], w_lo[:, c % RING, w],
                                  a_h[:, kt + k, :], a_l[:, kt + k, :],
                                  first and k == 0 and j % 2 == 0, last and k == 1)
            mm.then_inc(chunk_used, 1)

        def token_chunk(c, s, a_h, a_l, kt, first, last, i=None, step=0):
            pe.wait_ge(chunk_split, c + 1 if i is None else i * step + (c + 1))
            dst = flat(acc[s])
            for t in range(TT):
                for k in range(2):
                    o = dst[:, t * W:(t + 1) * W]
                    w = slice(k * W, (k + 1) * W)
                    sh, sl = a_h[:, kt + k, t * P:(t + 1) * P], a_l[:, kt + k, t * P:(t + 1) * P]
                    nc.tensor.matmul(o, sh, w_hi[:, c % RING, w], start=first and k == 0, stop=False, skip_group_check=True)
                    nc.tensor.matmul(o, sh, w_lo[:, c % RING, w], start=False, stop=False, skip_group_check=True)
                    mm = nc.tensor.matmul(o, sl, w_hi[:, c % RING, w], start=False, stop=last and k == 1, skip_group_check=True)
                if c == END - 1 and t < TT - 1:
                    mm.then_inc(tile0_sums, 1)
            mm.then_inc(chunk_used, 1)

        def column_sums(dst, src, n, k):
            for j in range(k):
                mm = nc.tensor.matmul(dst, ones[:], src[:, j, :n], start=j == 0, stop=j == k - 1, skip_group_check=True)
            return mm

        def token_sums(dst, src):
            for j in range(QD):
                for t in range(TT):
                    mm = nc.tensor.matmul(dst[:, 2 * j + t:2 * j + t + 1], src[:, j, t * P:(t + 1) * P], ones[:, 0:1],
                                          start=True, stop=True, skip_group_check=True)
            return mm

        def token_total(dst, src):
            for t in range(TT):
                mm = nc.tensor.matmul(dst[:, t:t + 1], src[:, t * P:(t + 1) * P], ones[:, 0:1],
                                      start=True, stop=True, skip_group_check=True)
            return mm

        def spread(n, dst, k, first=0):
            pe.wait_ge(rs_ready, n)
            for j in range(k):
                for t in range(TT):
                    i_ = 2 * j + t
                    mm = nc.tensor.matmul(dst[:, i_ * P:(i_ + 1) * P], ms[:, first + i_:first + i_ + 1].broadcast_to([P, P]), ident[:],
                                          start=True, stop=True, skip_group_check=True)
            mm.then_inc(rs_spread, 1)

        fa_flat = fa[:].rearrange("p b n -> p (b n)")
        fb_flat = fb[:].rearrange("p b n -> p (b n)")

        pe.wait_ge(consts, 1)
        pe.wait_ge(gain_landed, 16)
        nc.tensor.transpose(acc[0][:, 0, 0:KD], pst[0:KD, 5, :], ident[0:KD, 0:KD]).then_inc(gain_turned, 1)
        for q in range(4):
            dst = (fa if q % 2 == 0 else fb)[:].rearrange("p b (j s) -> p (b j) s", j=2)
            pe.wait_ge(x_landed[q], 16)
            if q >= 2:
                pe.wait_ge(xq_taken, q - 1)
            for j in range(QD):
                for t in range(TT):
                    k = 4 * q + j
                    mm = nc.tensor.transpose(dst[:, j, t * P:(t + 1) * P], xtok[:, t, k * P:(k + 1) * P], ident[:])
            mm.then_inc(xq_turned, 1)
        spread(1, flat(acc[1]), 1)

        levels = {GLA: 0}
        levels.update({GLA + 5 + 4 * n: n for n in range(1, 9)})

        def gla_level(n):
            if n == 0:
                wait_taken(pe, NUMBER["qk", 0])
                pe.wait_ge(yh_ready, 1)
                q, k = gqk[:, 0:2 * S], gqk[:, 2 * S:4 * S]
            else:
                pe.wait_ge(level_ready, n)
                q, k = lqk[:, 0:2 * S], lqk[:, 2 * S:4 * S]
            for par_ in range(2):
                r = slice(64 * par_, 64 * par_ + 64)
                for hp in range(2):
                    if n < 8:
                        for t in range(TT):
                            w = slice(hp * S + t * P, hp * S + (t + 1) * P)
                            m, tokens = 2 * hp + t, q[r, w]
                            if n:
                                tokens = tokens.rearrange("p (b two l) -> p b two l", two=2, l=1 << (n - 1))[:, :, 1, :]
                            cols = P // 2 if n else P
                            mm = nc.tensor.matmul(fb[:, par_, m * cols:(m + 1) * cols], k[r, w], tokens,
                                                  start=True, stop=True, skip_group_check=True)
                    else:
                        mm = nc.tensor.matmul(fb[:, par_, hp * P:(hp + 1) * P], k[r, hp * S:hp * S + P],
                                              q[r, hp * S + P:hp * S + S], start=True, stop=True, skip_group_check=True)
            mm.then_inc(level_sums, 1)

        def scores(h):
            if h == 0:
                pe.wait_ge(qk_normed, 4)
                pe.wait_ge(gla_r, 1)
                pe.wait_ge(unit_full, U_B + 1)
            if h >= 2:
                pe.wait_ge(sc_ready, h - 1)
            nc.tensor.matmul(fa[:, h % 2, P:3 * P], mq[:, h, P:S], mk[:, h, :], start=True, stop=True, skip_group_check=True)
            nc.tensor.matmul(fa[:, h % 2, 0:P], mq[:, h, 0:P], mk[:, h, 0:P], start=True, stop=True,
                             skip_group_check=True).then_inc(sc_sums, 1)

        def turn_probs(h):
            pe.wait_ge(pr_ready, h + 1)
            if h >= 1:
                pe.wait_ge(pT_ready, h)
            for b in range(3):
                mm = nc.tensor.transpose(fb[:, 0, b * P:(b + 1) * P], sc[:, h % 2, b * P:(b + 1) * P], ident[:])
            mm.then_inc(pr_turned, 1)

        def probs_v(h):
            pe.wait_ge(pT_ready, h + 1)
            if h == 0:
                for n in (0, 1):
                    wait_taken(pe, NUMBER["mv", n])
            else:
                pe.wait_ge(unit_full, U_C + h)
            nc.tensor.matmul(fb[:, 1, 0:S], mv[:, 0, h * HD:(h + 1) * HD], pT[:, h % 2, 0:S], start=True, stop=False, skip_group_check=True)
            nc.tensor.matmul(fb[:, 1, P:S], mv[:, 1, h * HD:(h + 1) * HD], pT[:, h % 2, S:S + P], start=False, stop=True,
                             skip_group_check=True).then_inc(pv_sums, 1)

        for c in range(UP1):
            name, g, j, n, number = GROUP_AT[c]
            s = number % 2
            if j == 0:
                if c == 0:
                    pe.wait_ge(gain_ready, 1)
                if c == FIRST["gate", 0]:
                    pe.wait_ge(rb_ready, 1)
                if number >= 2:
                    wait_taken(pe, number - 2)
            first, last = j == 0, j == n - 1
            if name in ("val", "gate", "qk", "gr", "mq", "mk", "mq2", "mk2", "gA", "gB", "gC"):
                if c < START:
                    pe.wait_ge(unit_split, U_H + c + 1)
                feature_chunk(c, s, h_hi, h_lo, 2 * j, first, last)
            elif name in ("gv", "mv"):
                token_chunk(c, s, h_hi, h_lo, 2 * j, first, last)
            elif name == "alow":
                pe.wait_ge(chunk_split, c + 1)
                for k in range(8):
                    w = slice(k * P, (k + 1) * P)
                    mm = products(acc[s][:, 0, :], w_hi[:, c % RING, w], w_lo[:, c % RING, w], h_hi[:, 8 * j + k, :],
                                  h_lo[:, 8 * j + k, :], first and k == 0, last and k == 7)
                mm.then_inc(chunk_used, 1)
            elif name == "yA":
                pe.wait_ge(unit_split, U_A + 1)
                feature_chunk(c, s, a_hi, a_lo, 2 * j, first, last)
            elif name == "yB":
                pe.wait_ge(unit_split, U_B + 1)
                feature_chunk(c, s, o_hi, o_lo, 2 * j, first, last)
            elif name == "yC":
                pe.wait_ge(unit_split, U_C + 2 * j + 2)
                feature_chunk(c, s, c_hi, c_lo, 2 * j, first, last)
            elif name == "wout":
                pe.wait_ge(unit_split, U_M + j // 2 + 1)
                feature_chunk(c, s, m_hi, m_lo, 2 * j, first, last)
            elif name == "ple":
                token_chunk(c, s, p_hi, p_lo, 0, True, True)

            if c == PAR:
                pe.wait_ge(par_landed, 16 * par_dmas)
                pe.wait_ge(xq_taken_act, 2)
                for b, n_rows in enumerate((R_ALL, TAPS * QD, 2 * FT, 2 * FT, 2 * FT)):
                    mm = nc.tensor.transpose(fb_flat[:, b * P:b * P + n_rows], pst[0:n_rows, b, :], ident[0:n_rows, 0:n_rows])
                mm.then_inc(par_turned, 1)
            if c == DECAY:
                wait_taken(pe, NUMBER["alow", 0])
                pe.wait_ge(par_ready, 1)
                for t in range(TT):
                    nc.tensor.matmul(fb[:, t, 0:S], alow[:, t * P:(t + 1) * P], wa2[:], start=True, stop=False, skip_group_check=True)
                    mm = nc.tensor.matmul(fb[:, t, 0:S], ones[0:1, :], brow[:], start=False, stop=True, skip_group_check=True)
                mm.then_inc(la_sums, 1)
            if c == DECAY + 8:
                pe.wait_ge(la_ready, 1)
                pe.wait_ge(consts, 2)
                for hp in range(2):
                    for t in range(TT):
                        mm = nc.tensor.matmul(fb[:, 0, hp * S + t * P:hp * S + (t + 1) * P],
                                              ex[:, t * S + hp * P:t * S + (hp + 1) * P], tri[:], start=True, stop=True, skip_group_check=True)
                mm.then_inc(bc_sums, 1)
            if c == CONV_LN:
                pe.wait_ge(conv_ready, 1)
                pe.wait_ge(bc_ready, 1)
                column_sums(fb[:, 0, 0:S], val, S, QD).then_inc(mean_sums, 1)
            if c == CONV_LN + 6:
                pe.wait_ge(xcsq_folded, 1)
                token_total(fb[:, 1, :], vsum).then_inc(var_sums, 1)
            if c == CONV_LN + 8:
                spread(3, fb[:, 1, :], 1, STAT_CONV)
            for k, name_ in enumerate(("mq", "mk", "mq2", "mk2")):
                if c == LAST[name_, 0] + 6:
                    wait_taken(pe, NUMBER[name_, 0])
                    if k:
                        pe.wait_ge(qk_normed, k)
                    token_sums(fa_flat, sqm).then_inc(norm_sums, 1)
                if c == LAST[name_, 0] + 8 and k % 2:
                    spread((4, 6)[k // 2], fa_flat, 4)
            if c in levels:
                gla_level(levels[c])
            if c == GLA + 42:
                pe.wait_ge(att_ready, 1)
                pe.wait_ge(qk_normed, 4)
                for h in range(GLA_HEADS):
                    a = 2 * (h % 2) + h // 2
                    o = slice((h % 2) * S, (h % 2) * S + S)
                    nc.tensor.matmul(fa[:, h // 2, o], gv[:, 0, h * P:(h + 1) * P], att[:, 2 * a:8 + a + 1:8 - a, :],
                                     start=h % 2 == 0, stop=False, skip_group_check=True)
                    mm = nc.tensor.matmul(fa[:, h // 2, o.start + P:o.stop], gv[:, 1, h * P:(h + 1) * P], att[:, 2 * a + 1, :],
                                          start=False, stop=True, skip_group_check=True)
                mm.then_inc(gla_o, 1)
            if c == GLA + 47:
                pe.wait_ge(gla_osq, 1)
                token_sums(fb_flat, tmpg[:].rearrange("p (j s) -> p j s", j=QD)).then_inc(gla_oss, 1)
            if c == GLA + 49:
                spread(7, fb_flat, 4)
            i = c - MOBA
            if i % 4 == 0 and 0 <= i < 4 * HEADS:
                scores(i // 4)
            if i % 4 == 1 and 5 <= i < 5 + 4 * HEADS:
                turn_probs((i - 5) // 4)
            if i % 4 == 3 and 7 <= i < 7 + 4 * HEADS:
                probs_v((i - 7) // 4)
            if c == FIRST["gC", 0] + 4:
                pe.wait_ge(p_landed, 16)
                pe.wait_ge(sc_ready, HEADS)
                for k in range(2):
                    for t in range(TT):
                        mm = nc.tensor.transpose(fa[:, 0, k * S + t * P:k * S + (t + 1) * P], ptok[:, t, k * P:(k + 1) * P], ident[:])
                mm.then_inc(p_turned, 1)
            if c == LAST["ple", 2]:
                pe.wait_ge(xsum_ready, 4)
                pe.wait_ge(unit_full, U_P + 1)
                token_total(fa_flat, sqsum).then_inc(xss, 1)
        pe.wait_ge(ms_ready, 8)
        spread(8, fa_flat, 1)

        def up(c0, pairs, group0, u_first):
            with pe.Fori(0, pairs) as i:
                for part in range(2):
                    pe.wait_ge(taken[part], i + group0 // 2)
                    for j in range(8):
                        if part == 0 and u_first and j % 2 == 0:
                            pe.wait_ge(unit_split, U_X1 + j // 2 + 1)
                        feature_chunk(c0 + 8 * part + j, part, h_hi, h_lo, 2 * j, j == 0, j == 7, i, 16)

        def down(c0, kt, group0, u0):
            n = kt // 2
            with pe.Fori(0, 2) as i:
                for half in range(2):
                    pe.wait_ge(taken[half], i + group0 // 2)
                    for j in range(n):
                        if half == 0 and j % 2 == 0:
                            pe.wait_ge(unit_split, u0 + j // 2 + 1)
                        feature_chunk(c0 + half * n + j, half, f_hi, f_lo, 2 * j, j == 0, j == n - 1, i, 2 * n)

        up(UP1, PAIRS1, NG_UP1, True)
        down(DOWN1, K1, NG_DOWN1, U_F)
        up(UP2, PAIRS2, NG_UP2, False)
        down(DOWN2, K2, NG_DOWN2, U_F + PAIRS1)
        for g in range(4):
            number = NG_PLEG + g
            wait_taken(pe, number - 2)
            for j in range(8):
                c = PLEG + 8 * g + j
                if g == 0 and j % 2 == 0:
                    pe.wait_ge(unit_split, U_X2 + j // 2 + 1)
                token_chunk(c, number % 2, h_hi, h_lo, 2 * j, j == 0, j == 7)
                if g == 1 and j < 4:
                    if j == 1:
                        pe.wait_ge(ms_ready, 9)
                    if j >= 2:
                        pe.wait_ge(x2_taken, j - 1)
                    dst = fb if j % 2 == 0 else fa
                    for t in range(TT):
                        for k in range(QD):
                            mm = nc.tensor.transpose(dst[:, t, k * P:(k + 1) * P], xT[:, 4 * j + k, t * P:(t + 1) * P], ident[:])
                    mm.then_inc(x2_turned, 1)
            if g == 0:
                pe.wait_ge(xsum_ready, 8)
                token_total(fa_flat, sqsum).then_inc(xss, 1)


    @block.scalar
    def _(act):
        A = nc.scalar
        act.dma_start(pst[0:KD, 5, :], norm_mix_g[0].rearrange("(r p) -> r p", p=P)).then_inc(gain_landed, 16)

        highs = [0]

        def earlier():
            act.wait_ge(chunk_high, highs[0])

        def high(c, i=None, step=0):
            highs[0] = c + 1 if i is None else i * step + (c + 1)
            if i is None:
                act.wait_ge(chunk_landed[c % RING], 16 * (c // RING + 1))
                if c >= RING:
                    act.wait_ge(chunk_used, c - RING + 1)
            else:
                act.wait_ge(chunk_landed[c % RING], i * (16 * step // RING) + 16 * (c // RING + 1))
                act.wait_ge(chunk_used, i * step + (c - RING + 1))
            A.copy(w_hi[:, c % RING, :], raw[:, c % RING, :]).then_inc(chunk_high, 1)

        def unit_to_high(u, src, dst, need=None):
            act.wait_ge(unit_full, u + 1 if need is None else need)
            A.copy(dst, src).then_inc(unit_high, 1)

        def unit(u):
            hi, _, n = unit_dst(u)
            unit_to_high(u, full[:, u % 2, 0:n, :], hi)

        act.wait_ge(consts, 1)
        A.activation(rB[:, 0:P], ones[:], ACT.Tanh).then_inc(act_step, 1)
        for q in range(4):
            act.wait_ge(x_landed[q], 16)
            for t in range(TT):
                last = A.activation(junk[:, 2 * q + t, :], xtok[:, t, q * W:(q + 1) * W], ACT.Square,
                                    accum_out=small[:, 4 * t + q:4 * t + q + 1])
        last.then_inc(ssq_ready, 1)
        high(0)
        for q in (2, 3):
            act.wait_ge(xq_turned, q + 1)
            A.copy(xT[:, 4 * q:4 * q + 4, :].rearrange("p j s -> p (j s)"),
                   (fa if q % 2 == 0 else fb)[:].rearrange("p b n -> p (b n)")).then_inc(xq_taken_act, 1)
        for c in range(START):
            if c:
                high(c)
            unit(U_H + c)

        def take(number, dst, src, scale=None):
            if scale is None:
                return A.copy(dst, src).then_inc(taken[number % 2], 1)
            return A.mul(dst, src, scale).then_inc(taken[number % 2], 1)

        for c in range(START, UP1 + 12):
            high(c)
            e = c - RING
            if c - 3 in GROUP_AT and GROUP_AT[c - 3][0] == "ple":
                e = c - 3
            if e in GROUP_AT and e == LAST[GROUP_AT[e][:2]] and not (GROUP_AT[e][0] == "ple" and e == c - RING):
                earlier()
                name, g, _, _, number = GROUP_AT[e]
                a = acc[number % 2]
                if name == "ple":
                    act.wait_ge(chunk_used, e + 1)
                if name == "val":
                    act.wait_ge(unit_split, U_H + 8)
                    take(number, val[:], a[:], 0.5)
                elif name == "gate":
                    A.activation(tanhg[:], a[:], ACT.Tanh, scale=0.5).then_inc(taken[number % 2], 1)
                elif name == "qk":
                    A.mul(gqk[:, 0:2 * S], flat(a)[:, 0:2 * S], GLA_DK ** -0.5)
                    take(number, gqk[:, 2 * S:4 * S], flat(a)[:, 2 * S:4 * S])
                elif name == "alow":
                    take(number, alow[:], a[0:GLA_RANK, 0, :])
                elif name == "gv":
                    take(number, flat(gv), flat(a))
                elif name == "gr":
                    A.activation(tmpg[:], flat(a), ACT.Tanh, scale=0.5)
                    take(number, gr[:], a[:], 0.5)
                elif name in ("mq", "mk", "mq2", "mk2"):
                    k = ("mq", "mk", "mq2", "mk2").index(name)
                    dst = (mq, mk)[k % 2]
                    A.mul(dst[:, 4 * (k // 2):4 * (k // 2) + 4, :], a[:], par[:, R_Q + k % 2:R_Q + k % 2 + 1])
                    if k:
                        act.wait_ge(norm_sums, k)
                    A.activation(sqm[:], a[:], ACT.Square).then_inc(taken[number % 2], 1)
                elif name == "mv":
                    take(number, mv[:, :, g * W:(g + 1) * W], flat(a).rearrange("p (t n) -> p t n", t=TT))
                elif name == "yA":
                    take(number, merged[:, 4 * g:4 * g + 4, :], a[:], 0.5)
                elif name in ("yB", "yC"):
                    if name == "yB" and g == 0:
                        act.wait_ge(att_ready, 1)
                    if name == "yC":
                        act.wait_ge(gate_merged, 4 + g + 1)
                    take(number, yb[:, 4 * g:4 * g + 4, :], a[:], 0.5)
                elif name in ("gA", "gB", "gC"):
                    b = "ABC".index(name[1])
                    if b == 2 and g:
                        act.wait_ge(unit_full, U_M + g)
                    elif 4 * b + g:
                        act.wait_ge(gate_merged, 4 * b + g)
                    for j in range(QD):
                        col = R_BG + 16 * b + 4 * g + j
                        last = A.activation(gt[:, j, :], a[:, j, :], ACT.Tanh, bias=parh[:, col:col + 1], scale=0.5)
                    last.then_inc(taken[number % 2], 1)
                elif name == "ple":
                    take(number, ple[:, :, g * W:(g + 1) * W], flat(a).rearrange("p (t n) -> p t n", t=TT), 0.5)
            if c == DECAY + 5:
                earlier()
                act.wait_ge(la_abs, 1)
                A.activation(lqk[:, 0:2 * S], lqk[:, 0:2 * S], ACT.Exp, scale=-1.0).then_inc(act_step, 1)
                act.wait_ge(act_step, 2)
                A.activation(lqk[:, 0:2 * S], lqk[:, 0:2 * S], ACT.Ln, bias=1.0).then_inc(la_exp, 1)
            if c == DECAY + 12:
                earlier()
                act.wait_ge(bc_sums, 1)
                A.copy(bc[:], fb[:, 0, :]).then_inc(bc_ready, 1)
            if c == CONV_LN + 5:
                earlier()
                act.wait_ge(xc_ready, 1)
                A.activation(tanhg[:], val[:], ACT.Square).then_inc(xcsq_ready, 1)
            if c == GLA:
                earlier()
                act.wait_ge(yh_ready, 1)
                A.activation(tanhg[:], val[:], ACT.Tanh).then_inc(ytanh_ready, 1)
            if c == GLA + 3:
                earlier()
                unit(U_A)
            for n in range(1, 9):
                if c == GLA + 6 + 4 * n:
                    earlier()
                    act.wait_ge(exps_wanted, n)
                    A.activation(ex[:], ex[:], ACT.Exp).then_inc(exps_ready, 1)
            if c == GLA + 46:
                earlier()
                act.wait_ge(gla_o, 1)
                A.activation(tmpg[:], fa[:].rearrange("p b n -> p (b n)"), ACT.Square).then_inc(gla_osq, 1)
            if c == GLA + 54:
                earlier()
                unit(U_B)
            i = c - MOBA
            if i % 4 == 2 and 6 <= i < 6 + 4 * HEADS:
                h = (i - 6) // 4
                earlier()
                act.wait_ge(sc_ready, h + 1)
                b = 2 + 6 * (h % 2)
                for t, w in ((0, slice(0, P)), (1, slice(P, 3 * P))):
                    last = A.activation(sc[:, h % 2, w], sc[:, h % 2, w], ACT.Exp, bias=small[:, b + t:b + t + 1],
                                        scale=rq[:, h // 4, 2 * (h % 4) + t:2 * (h % 4) + t + 1],
                                        accum_out=small[:, b + 2 + t:b + 3 + t])
                last.then_inc(sc_exp, 1)
            if i % 4 == 1 and 9 <= i < 9 + 4 * HEADS:
                h = (i - 9) // 4
                earlier()
                act.wait_ge(pr_turned, h + 1)
                if h >= 2:
                    act.wait_ge(pv_sums, h - 1)
                A.copy(pT[:, h % 2, :], fb[:, 0, 0:3 * P]).then_inc(pT_ready, 1)
            if i % 4 == 0 and 12 <= i < 12 + 4 * HEADS:
                earlier()
                unit(U_C + (i - 12) // 4)
            if c == FIRST["gC", 0] + 9:
                earlier()
                unit(U_P)
            for g in range(4):
                if c == LAST["gC", g] + 5:
                    earlier()
                    unit(U_M + g)
                if c == LAST["wout", g] + 4:
                    earlier()
                    unit(U_X1 + g)
                if c == LAST["wout", g] + 3:
                    earlier()
                    act.wait_ge(x_new, g + 1)
                    if g:
                        act.wait_ge(xsum_ready, g)
                    A.activation(sqx[:], xT[:, 4 * g:4 * g + 4, :], ACT.Square).then_inc(xsq_ready, 1)

        def taps0(k, src, dst, col, i, need):
            act.wait_ge(taken[k], need)
            earlier()
            for j in range(QD):
                last = A.mul(dst[:, j, :], src[:, j, 2:2 + S], fw[:, 2, bass.ds(i * QD + (col + j), 1)])
            last.then_inc(tap_ready, 1)

        def up(c0, pairs, group0, pair0, u0):
            with act.Fori(0, pairs) as i:
                highs[0] = i * 16 + (c0 + 12)
                taps0(0, upg, cg, 4 * pair0, i, i + (group0 // 2 + 1))
                for k in range(12, 15):
                    high(c0 + k, i, 16)
                act.wait_ge(cg_ready, i + (pair0 + 1))
                earlier()
                A.activation(tg[:], cg[:], ACT.Tanh).then_inc(tg_ready, 1)
                for k in range(15, 20):
                    high(c0 + k, i, 16)
                taps0(1, upv, cv, FT + 4 * pair0, i, i + (group0 // 2 + 1))
                for k in range(20, 23):
                    high(c0 + k, i, 16)
                earlier()
                unit_to_high(0, full[:, 0, :, :], f_hi[:, bass.ds(i * QD, QD), :], need=i + (u0 + 1))
                for k in range(23, 28):
                    high(c0 + k, i, 16)

        def down(c0, kt):
            n = kt // 2
            with act.Fori(0, 2) as i:
                for k in range(12, 12 + 2 * n):
                    high(c0 + k, i, 2 * n)

        up(UP1, PAIRS1, NG_UP1, 0, U_F)
        down(DOWN1, K1)
        up(UP2, PAIRS2, NG_UP2, PAIRS1, U_F + PAIRS1)
        n = K2 // 2
        with act.Fori(0, 2) as i:
            for k in range(12, 12 + 2 * n):
                high(DOWN2 + k, i, 2 * n)
                for half in range(2):
                    if k == half * n + n + 4:
                        earlier()
                        unit_to_high(0, full[:, half, :, :], h_hi[:, bass.ds(i * 8 + 4 * half, 4), :],
                                     need=i * 2 + (U_X2 + half + 1))
                        act.wait_ge(xsum_ready, i * 2 + (4 + half))
                        A.activation(sqx[:], xT[:, bass.ds(i * 8 + 4 * half, 4), :], ACT.Square).then_inc(xsq_ready, 1)
        for c in range(PLEG + 12, END + 4):
            if c < END:
                high(c)
            earlier()
            q = c - PLEG - 12
            if q < 4:
                act.wait_ge(x2_turned, q + 1)
                A.copy(x2tok[:, :, q * W:(q + 1) * W], (fb if q % 2 == 0 else fa)[:]).then_inc(x2_taken, 1)
            for g in range(3):
                if c == PLEG + 8 * g + (13 if g == 0 else 11):
                    number = NG_PLEG + g
                    act.wait_ge(chunk_used, PLEG + 8 * g + 8)
                    act.wait_ge(r2_ready, 1)
                    if g:
                        act.wait_ge(pg_ready, g)
                    for t in range(TT):
                        last = A.activation(gt2[:, t, :], flat(acc[number % 2])[:, t * W:(t + 1) * W], ACT.Tanh,
                                            scale=small[:, 14 - t:15 - t])
                    last.then_inc(taken[number % 2], 1)
        act.wait_ge(pg_ready, 3)
        for t in range(TT):
            if t == 0:
                act.wait_ge(tile0_sums, 1)
            else:
                act.wait_ge(chunk_used, END)
            A.activation(gt2[:, t, :], flat(acc[(NG_PLEG + 3) % 2])[:, t * W:(t + 1) * W], ACT.Tanh,
                         scale=small[:, 14 - t:15 - t]).then_inc(tile_gate, 1)

    @block.vector
    def _(dve):
        V = nc.vector
        steps = [0]

        def step(ins):
            ins.then_inc(dve_step, 1)
            steps[0] += 1

        def sync():
            dve.wait_ge(dve_step, steps[0])

        splits = [0]

        def earlier():
            dve.wait_ge(chunk_split, splits[0])

        def split(c, i=None, step=0):
            splits[0] = c + 1 if i is None else i * step + (c + 1)
            dve.wait_ge(chunk_high, c + 1 if i is None else i * step + (c + 1))
            V.tensor_tensor(w_lo[:, c % RING, :], raw[:, c % RING, :], w_hi[:, c % RING, :].bitcast(F32),
                            ALU.subtract).then_inc(chunk_split, 1)

        def unit(u):
            hi, lo, n = unit_dst(u)
            dve.wait_ge(unit_high, u + 1)
            V.tensor_tensor(lo, full[:, u % 2, 0:n, :], hi.bitcast(F32), ALU.subtract).then_inc(unit_split, 1)

        def quad(a):
            return a.unsqueeze(1).broadcast_to([P, QD, S])

        def fold(dst, src):
            return V.tensor_reduce(dst, src.rearrange("p j s -> p s j"), AX_X, ALU.add)

        dve.wait_ge(gain_turned, 1)
        V.tensor_copy(par[:, 0:KD], acc[0][:, 0, 0:KD]).then_inc(gain_ready, 1)
        for q in range(2):
            dve.wait_ge(xq_turned, q + 1)
            V.tensor_copy(xT[:, 4 * q:4 * q + 4, :].rearrange("p j s -> p (j s)"),
                          (fa if q % 2 == 0 else fb)[:].rearrange("p b n -> p (b n)")).then_inc(xq_taken, 1)
        dve.wait_ge(ssq_ready, 1)
        step(V.tensor_reduce(ms[:, 0:TT], small[:, 0:4 * TT].rearrange("p (t q) -> p t q", t=TT), AX_X, ALU.add))
        sync()
        V.tensor_scalar(ms[:, 0:TT], ms[:, 0:TT], 1.0 / D, EPS, ALU.mult, ALU.add).then_inc(ms_ready, 1)
        split(0)
        dve.wait_ge(rs_spread, 1)
        V.tensor_copy(rB[:], acc[1][:, 0, :]).then_inc(rb_ready, 1)
        dve.wait_ge(rb_ready, 1)
        dve.wait_ge(gain_ready, 1)
        dve.wait_ge(xq_taken, 2)
        for c in range(START):
            if c >= 4:
                dve.wait_ge(xq_taken_act, c // 2 - 1)
            if c >= 2:
                dve.wait_ge(unit_split, c - 1)
            for j in range(2):
                k = 2 * c + j
                last = V.scalar_tensor_tensor(full[:, c % 2, j, :], xT[:, k, :], par[:, R_MIX + k:R_MIX + k + 1],
                                              rB[:], ALU.mult, ALU.mult)
            last.then_inc(unit_full, 1)
            if c:
                split(c)
            unit(U_H + c)

        def glu():
            wait_taken(dve, NUMBER["val", 0])
            wait_taken(dve, NUMBER["gate", 0])
            V.memset(apad[:, :, 0:TAPS - 1], 0.0)
            step(V.scalar_tensor_tensor(apad[:, :, TAPS - 1:], tanhg[:], 1.0, val[:], ALU.add, ALU.mult))

        def conv_tap(k):
            sync()
            for j in range(QD):
                src = apad[:, j, k:k + S]
                w = cw[:, k * QD + j:k * QD + j + 1]
                if k == 0:
                    last = V.tensor_scalar(val[:, j, :], src, w, par[:, R_CB + j:R_CB + j + 1], ALU.mult, ALU.add)
                else:
                    last = V.scalar_tensor_tensor(val[:, j, :], src, w, val[:, j, :], ALU.mult, ALU.add)
            if k < TAPS - 1:
                step(last)
            else:
                last.then_inc(conv_ready, 1)

        def level_exponents(n):
            half = 1 << (n - 1)
            if n == 1:
                dve.wait_ge(bc_ready, 1)
            if n < 8:
                b = bc[:].rearrange("p (b two l) -> p b two l", two=2, l=half)
                e = ex[:].rearrange("p (b two l) -> p b two l", two=2, l=half)
                end = b[:, :, 0, half - 1:half].broadcast_to([P, 2 * S // (2 * half), half])
                V.tensor_tensor(e[:, :, 0, :], end, b[:, :, 0, :], ALU.subtract)
                if half < GLA_CHUNK:
                    last = V.tensor_tensor(e[:, :, 1, :], b[:, :, 1, :], end, ALU.subtract)
                else:
                    last = V.tensor_copy(e[:, :, 1, :], b[:, :, 1, :])
                last.then_inc(exps_wanted, 1)
                return
            b = bc[:].rearrange("p (h c l) -> p h c l", h=2, l=GLA_CHUNK)
            e = ex[:].rearrange("p (h c l) -> p h c l", h=2, l=GLA_CHUNK)

            V.tensor_tensor(e[:, :, 1, :], b[:, :, 1, GLA_CHUNK - 1:GLA_CHUNK].broadcast_to([P, 2, GLA_CHUNK]), b[:, :, 1, :], ALU.subtract)
            V.tensor_tensor(e[:, :, 0, :], b[:, :, 0, GLA_CHUNK - 1:GLA_CHUNK].broadcast_to([P, 2, GLA_CHUNK]), b[:, :, 0, :], ALU.subtract)
            V.tensor_copy(e[:, :, 2, :], b[:, :, 2, :])
            step(V.tensor_tensor(e[:, :, 3, :], b[:, :, 3, :], b[:, :, 2, GLA_CHUNK - 1:GLA_CHUNK].broadcast_to([P, 2, GLA_CHUNK]), ALU.add))
            sync()
            V.tensor_tensor(e[:, :, 0, :], e[:, :, 0, :], b[:, :, 1, GLA_CHUNK - 1:GLA_CHUNK].broadcast_to([P, 2, GLA_CHUNK]), ALU.add).then_inc(exps_wanted, 1)

        def level_scale(n):
            dve.wait_ge(exps_ready, n)
            dve.wait_ge(level_sums, n)
            V.tensor_tensor(lqk[:, 0:2 * S], gqk[:, 0:2 * S], ex[:], ALU.mult)
            V.tensor_tensor(lqk[:, 2 * S:4 * S], gqk[:, 2 * S:4 * S], ex[:], ALU.mult).then_inc(level_ready, 1)

        def level_add(n):
            dve.wait_ge(level_sums, n + 1)
            if n == 8:
                V.tensor_copy(att[:, 8:12, :].rearrange("p (b h) t -> p b h t", b=2),
                              fb[:, :, 0:2 * P].rearrange("p b (h t) -> p b h t", h=2)).then_inc(att_ready, 1)
                return
            if n == 0:
                step(V.tensor_tensor(att[:, 0:8, :].rearrange("p (b m) t -> p b m t", b=2),
                                     fb[:].rearrange("p b (m t) -> p b m t", t=P),
                                     ident[:].unsqueeze(1).unsqueeze(1).broadcast_to([P, 2, 4, P]), ALU.mult))
                return
            cols, half = P // 2, 1 << (n - 1)
            if n == 1:
                dve.wait_ge(consts, 2)
            step(V.tensor_tensor(tmpg[:, 0:2 * S].rearrange("p (b m t) -> p b m t", b=2, t=cols),
                                 fb[:, :, 0:4 * cols].rearrange("p b (m t) -> p b m t", t=cols),
                                 masks[:, n - 1, :].unsqueeze(1).unsqueeze(1).broadcast_to([P, 2, 4, cols]), ALU.mult))
            sync()
            dst = att[:, 0:8, :].rearrange("p m t -> p (m t)").rearrange("p (x two l) -> p x two l", two=2, l=half)[:, :, 1, :]
            step(V.tensor_tensor(dst, dst, tmpg[:, 0:2 * S].rearrange("p (x l) -> p x l", l=half), ALU.add))

        free = [c for c in range(GLU + 1, CONV_LN) if c not in (DECAY + 4, DECAY + 6, DECAY + 12, SILU_R)]
        tap_at = dict(zip(free, range(TAPS), strict=True))
        norm_at = {}
        for k, name_ in enumerate(("mq", "mk", "mq2", "mk2")):
            norm_at[LAST[name_, 0] + 10] = (k, "ms")
            norm_at[LAST[name_, 0] + 12] = (k, "scale")
        for c in range(START, UP1 + 12):
            split(c)
            if c == PAR + 4:
                dve.wait_ge(par_turned, 1)
                flat0 = fb[:].rearrange("p b n -> p (b n)")
                V.tensor_copy(par[:, KD:R_ALL], flat0[:, KD:R_ALL])
                V.tensor_scalar(parh[:], flat0[:, 0:R_ALL], 0.5, None, ALU.mult)
                V.tensor_copy(cw[:], flat0[:, P:P + TAPS * QD])
                fsrc = flat0[:, 2 * P:5 * P].rearrange("p (w n) -> p w n", w=FFN_TAPS)
                V.tensor_scalar(fw[:, :, 0:FT], fsrc[:, :, 0:FT], 0.5, None, ALU.mult)
                V.tensor_copy(fw[:, :, FT:2 * FT], fsrc[:, :, FT:2 * FT]).then_inc(par_ready, 1)
            if c == GLU:
                dve.wait_ge(par_ready, 1)
                earlier()
                glu()
            if c in tap_at:
                earlier()
                conv_tap(tap_at[c])
            if c == DECAY + 4:
                earlier()
                dve.wait_ge(la_sums, 1)
                z = fb[:, :, 0:S]
                m, n_ = ex[:].rearrange("p (t n) -> p t n", t=TT), lqk[:, 0:2 * S].rearrange("p (t n) -> p t n", t=TT)
                V.tensor_scalar(m, z, 0.0, None, ALU.min)
                step(V.tensor_scalar(n_, z, 0.0, None, ALU.max))
                sync()
                V.tensor_tensor(lqk[:, 0:2 * S], lqk[:, 0:2 * S], ex[:], ALU.subtract).then_inc(la_abs, 1)
            if c == DECAY + 6:
                earlier()
                dve.wait_ge(la_exp, 1)
                V.tensor_tensor(ex[:], ex[:], lqk[:, 0:2 * S], ALU.subtract).then_inc(la_ready, 1)
            if c == SILU_R:
                earlier()
                wait_taken(dve, NUMBER["gr", 0])
                step(V.scalar_tensor_tensor(gr[:].rearrange("p j s -> p (j s)"), tmpg[:], 1.0,
                                            gr[:].rearrange("p j s -> p (j s)"), ALU.add, ALU.mult))
            if c == CONV_LN + 6:
                earlier()
                dve.wait_ge(xcsq_ready, 1)
                fold(vsum[:], tanhg[:]).then_inc(xcsq_folded, 1)
            if c == CONV_LN + 4:
                earlier()
                dve.wait_ge(mean_sums, 1)
                V.scalar_tensor_tensor(val[:], quad(fb[:, 0, 0:S]), -1.0 / CONV_CH, val[:], ALU.mult, ALU.add).then_inc(xc_ready, 1)
            if c in norm_at:
                k, what = norm_at[c]
                earlier()
                if what == "ms":
                    dve.wait_ge(norm_sums, k + 1)
                    V.tensor_scalar(ms[:, 0:8], fa[:, 0, 0:8], 1.0 / HD, EPS, ALU.mult, ALU.add).then_inc(ms_ready, 1)
                elif k % 2 == 0:
                    dve.wait_ge(rs_ready, (2, 5)[k // 2])
                    V.tensor_scalar(rq[:, k // 2, :], ms[:, 0:8], HD ** -0.5, None, ALU.mult).then_inc(qk_normed, 1)
                else:
                    dve.wait_ge(rs_spread, (3, 4)[k // 2])
                    dst = mk[:, 4 * (k // 2):4 * (k // 2) + 4, :]
                    V.tensor_tensor(dst, dst, fa[:].rearrange("p b (j s) -> p (b j) s", j=2), ALU.mult).then_inc(qk_normed, 1)
            if c == CONV_LN + 10:
                earlier()
                dve.wait_ge(var_sums, 1)
                V.tensor_scalar(ms[:, STAT_CONV:STAT_CONV + TT], fb[:, 1, 0:TT], 1.0 / CONV_CH, EPS, ALU.mult, ALU.add).then_inc(ms_ready, 1)
            if c == CONV_LN + 12:
                earlier()
                dve.wait_ge(rs_spread, 2)
                dve.wait_ge(xc_ready, 1)
                step(V.tensor_tensor(val[:], val[:], quad(fb[:, 1, 0:S]), ALU.mult))
                sync()
                for j in range(QD):
                    last = V.tensor_scalar(val[:, j, :], val[:, j, :], parh[:, R_LG + j:R_LG + j + 1],
                                           parh[:, R_LB + j:R_LB + j + 1], ALU.mult, ALU.add)
                last.then_inc(yh_ready, 1)
            if c == GLA + 2:
                earlier()
                dve.wait_ge(ytanh_ready, 1)
                V.scalar_tensor_tensor(full[:, U_A % 2, :, :], tanhg[:], 1.0, val[:], ALU.add, ALU.mult).then_inc(unit_full, 1)
            if c == GLA + 4:
                earlier()
                unit(U_A)
            if c == GLA + 5:
                earlier()
                level_add(0)
            for n in range(1, 9):
                if c == GLA + 6 + 4 * n:
                    earlier()
                    level_exponents(n)
                if c == GLA + 7 + 4 * n:
                    earlier()
                    level_scale(n)
                if c == GLA + 9 + 4 * n:
                    earlier()
                    level_add(n)
            if c == GLA + 47:
                earlier()
                dve.wait_ge(gla_o, 1)
                dve.wait_ge(gla_osq, 1)
                V.scalar_tensor_tensor(gr[:].rearrange("p j s -> p (j s)"), fa[:].rearrange("p b n -> p (b n)"),
                                       par[:, R_GLA:R_GLA + 1], gr[:].rearrange("p j s -> p (j s)"),
                                       ALU.mult, ALU.mult).then_inc(gla_r, 1)
            if c == GLA + 51:
                earlier()
                dve.wait_ge(gla_oss, 1)
                V.tensor_scalar(ms[:, 0:8], fb[:, 0, 0:8], 1.0 / GLA_DV, EPS, ALU.mult, ALU.add).then_inc(ms_ready, 1)
            if c == GLA + 53:
                earlier()
                dve.wait_ge(rs_spread, 5)
                dve.wait_ge(gla_r, 1)
                V.tensor_tensor(full[:, U_B % 2, :, :], gr[:], fb[:].rearrange("p b (j s) -> p (b j) s", j=2), ALU.mult).then_inc(unit_full, 1)
            if c == GLA + 55:
                earlier()
                unit(U_B)
            i = c - MOBA
            if i % 4 == 1 and 5 <= i < 5 + 4 * HEADS:
                h = (i - 5) // 4
                earlier()
                s_ = sc[:, h % 2, :]
                b = 2 + 6 * (h % 2)
                dve.wait_ge(sc_sums, h + 1)
                step(V.tensor_tensor(s_, fa[:, h % 2, 0:3 * P], cmask[:].rearrange("p a b -> p (a b)"), ALU.add))
                sync()
                V.tensor_reduce(small[:, b:b + 1], s_[:, 0:P], AX_X, ALU.max)
                step(V.tensor_reduce(small[:, b + 1:b + 2], s_[:, P:3 * P], AX_X, ALU.max))
                sync()
                V.scalar_tensor_tensor(small[:, b:b + 2], small[:, b:b + 2], -1.0,
                                       rq[:, h // 4, 2 * (h % 4):2 * (h % 4) + 2], ALU.mult, ALU.mult).then_inc(sc_ready, 1)
            if i % 4 == 3 and 7 <= i < 7 + 4 * HEADS:
                h = (i - 7) // 4
                earlier()
                b = 4 + 6 * (h % 2)
                dve.wait_ge(sc_exp, h + 1)
                step(V.reciprocal(small[:, b:b + 2], small[:, b:b + 2]))
                sync()
                V.tensor_scalar(sc[:, h % 2, 0:P], sc[:, h % 2, 0:P], small[:, b:b + 1], None, ALU.mult)
                V.tensor_scalar(sc[:, h % 2, P:3 * P], sc[:, h % 2, P:3 * P], small[:, b + 1:b + 2], None, ALU.mult).then_inc(pr_ready, 1)
            if i % 4 == 3 and 11 <= i < 11 + 4 * HEADS:
                h = (i - 11) // 4
                earlier()
                dve.wait_ge(pv_sums, h + 1)
                V.tensor_copy(full[:, (U_C + h) % 2, 0, :], fb[:, 1, 0:S]).then_inc(unit_full, 1)
            if i % 4 == 0 and 12 <= i < 12 + 4 * HEADS:
                earlier()
                unit(U_C + (i - 12) // 4)
            for b in range(3):
                for g in range(4):
                    name = "g" + "ABC"[b]
                    q = slice(4 * g, 4 * g + 4)
                    if c == LAST[name, g] + (6 if b < 2 else 5):
                        earlier()
                        wait_taken(dve, NUMBER[name, g])
                        if b == 0:
                            wait_taken(dve, NUMBER["yA", g])
                            V.scalar_tensor_tensor(merged[:, q, :], gt[:], 1.0, merged[:, q, :], ALU.add, ALU.mult).then_inc(gate_merged, 1)
                        else:
                            wait_taken(dve, NUMBER["yB" if b == 1 else "yC", g])
                            step(V.scalar_tensor_tensor(yb[:, q, :], gt[:], 1.0, yb[:, q, :], ALU.add, ALU.mult))
                            sync()
                            if b == 1:
                                V.tensor_tensor(merged[:, q, :], merged[:, q, :], yb[:, q, :], ALU.add).then_inc(gate_merged, 1)
                            else:
                                V.tensor_tensor(full[:, (U_M + g) % 2, :, :], merged[:, q, :], yb[:, q, :], ALU.add).then_inc(unit_full, 1)
                    if b == 2 and c == LAST[name, g] + 6:
                        earlier()
                        unit(U_M + g)
            if c == FIRST["gC", 0] + 8:
                earlier()
                dve.wait_ge(p_turned, 1)
                V.tensor_copy(full[:, U_P % 2, 0:2, :].rearrange("p j s -> p (j s)"), fa[:, 0, :]).then_inc(unit_full, 1)
            if c == FIRST["gC", 0] + 10:
                earlier()
                unit(U_P)
            for g in range(4):
                if c == LAST["wout", g] + 3:
                    earlier()
                    number = NUMBER["wout", g]
                    q = slice(4 * g, 4 * g + 4)
                    dve.wait_ge(chunk_used, LAST["wout", g] + 1)
                    V.tensor_tensor(xT[:, q, :], xT[:, q, :], acc[number % 2][:], ALU.add).then_inc(taken[number % 2], 1)
                    wait_taken(dve, number)
                    for j in range(QD):
                        last = V.tensor_scalar(full[:, (U_X1 + g) % 2, j, :], xT[:, 4 * g + j, :],
                                               par[:, R_FFN + 4 * g + j:R_FFN + 4 * g + j + 1], None, ALU.mult)
                        if j == 0:
                            last.then_inc(x_new, 1)
                    last.then_inc(unit_full, 1)
                    dve.wait_ge(xsq_ready, g + 1)
                    if g == 0:
                        fold(sqsum[:], sqx[:]).then_inc(xsum_ready, 1)
                    else:
                        step(fold(sqfold[:], sqx[:]))
                        sync()
                        dve.wait_ge(xsum_ready, g)
                        V.tensor_tensor(sqsum[:], sqsum[:], sqfold[:], ALU.add).then_inc(xsum_ready, 1)
                if c == LAST["wout", g] + 4:
                    earlier()
                    unit(U_X1 + g)
            if c == UP1 + 1:
                earlier()
                dve.wait_ge(xss, 1)
                V.tensor_scalar(ms[:, 0:TT], fa[:, 0, 0:TT], 1.0 / D, EPS, ALU.mult, ALU.add).then_inc(ms_ready, 1)
            if c == UP1 + 3:
                earlier()
                dve.wait_ge(rs_spread, 6)
                step(V.tensor_copy(rB[:], fa[:, 0, 0:S]))
                V.memset(upg[:, :, 0:2], 0.0)
                step(V.memset(upv[:, :, 0:2], 0.0))
                sync()

        d0 = steps[0]

        def up(c0, pairs, pair0, u0, d0):
            with dve.Fori(0, pairs) as i:
                def conv(src, dst, col, taps):
                    dve.wait_ge(tap_ready, i * 2 + taps)
                    for j in range(QD):
                        last = V.scalar_tensor_tensor(dst[:, j, :], src[:, j, 1:1 + S], fw[:, 1, bass.ds(i * QD + (col + j), 1)],
                                                      dst[:, j, :], ALU.mult, ALU.add)
                    last.then_inc(dve_step, 1)

                def conv2(src, dst, col, count, done):
                    dve.wait_ge(dve_step, i * 2 + count)
                    for j in range(QD):
                        last = V.scalar_tensor_tensor(dst[:, j, :], src[:, j, 0:S], fw[:, 0, bass.ds(i * QD + (col + j), 1)],
                                                      dst[:, j, :], ALU.mult, ALU.add)
                    last.then_inc(done, 1)

                dve.wait_ge(chunk_split, i * 16 + (c0 + 12))
                dve.wait_ge(chunk_used, i * 16 + (c0 + 8))
                V.tensor_tensor(upg[:, :, 2:], acc[0][:], quad(rB[:]), ALU.mult).then_inc(taken[0], 1)
                split(c0 + 12, i, 16)
                conv(upg, cg, 4 * pair0, 2 * pair0 + 1)
                split(c0 + 13, i, 16)
                conv2(upg, cg, 4 * pair0, d0 + 1, cg_ready)
                split(c0 + 14, i, 16)
                split(c0 + 15, i, 16)
                dve.wait_ge(tg_ready, i + (pair0 + 1))
                dve.wait_ge(cg_ready, i + (pair0 + 1))
                V.scalar_tensor_tensor(cg[:], tg[:], 1.0, cg[:], ALU.add, ALU.mult)
                for k in range(16, 20):
                    split(c0 + k, i, 16)
                earlier()
                dve.wait_ge(chunk_used, i * 16 + (c0 + 16))
                V.tensor_tensor(upv[:, :, 2:], acc[1][:], quad(rB[:]), ALU.mult).then_inc(taken[1], 1)
                split(c0 + 20, i, 16)
                conv(upv, cv, FT + 4 * pair0, 2 * pair0 + 2)
                split(c0 + 21, i, 16)
                conv2(upv, cv, FT + 4 * pair0, d0 + 2, cv_ready)
                split(c0 + 22, i, 16)
                earlier()
                dve.wait_ge(cv_ready, i + (pair0 + 1))
                V.tensor_tensor(full[:, 0, :, :], cg[:], cv[:], ALU.mult).then_inc(unit_full, 1)
                split(c0 + 23, i, 16)
                earlier()
                dve.wait_ge(unit_high, i + (u0 + 1))
                V.tensor_tensor(f_lo[:, bass.ds(i * QD, QD), :], full[:, 0, :, :], f_hi[:, bass.ds(i * QD, QD), :].bitcast(F32),
                                ALU.subtract).then_inc(unit_split, 1)
                for k in range(24, 28):
                    split(c0 + k, i, 16)
            return d0 + 2 * pairs

        d0 = up(UP1, PAIRS1, 0, U_F, d0)
        n = K1 // 2
        with dve.Fori(0, 2) as i:
            for k in range(12, 12 + 2 * n):
                split(DOWN1 + k, i, 2 * n)
                for half in range(2):
                    if k == half * n + n + 3:
                        earlier()
                        dve.wait_ge(chunk_used, i * (2 * n) + (DOWN1 + half * n + n))
                        v = xT[:, bass.ds(i * 8 + 4 * half, 4), :]
                        V.tensor_tensor(v, v, acc[half][:], ALU.add).then_inc(taken[half], 1)
        d0 = up(UP2, PAIRS2, PAIRS1, U_F + PAIRS1, d0)
        dve.wait_ge(xss, 1)
        earlier()
        V.memset(sqsum[:], 0.0).then_inc(dve_step, 1)
        d0 += 1
        dve.wait_ge(dve_step, d0)
        n = K2 // 2
        with dve.Fori(0, 2) as i:
            for k in range(12, 12 + 2 * n):
                split(DOWN2 + k, i, 2 * n)
                for half in range(2):
                    if k == half * n + n + 3:
                        earlier()
                        dve.wait_ge(chunk_used, i * (2 * n) + (DOWN2 + half * n + n))
                        v = xT[:, bass.ds(i * 8 + 4 * half, 4), :]
                        V.tensor_tensor(v, v, acc[half][:], ALU.add).then_inc(taken[half], 1)
                        dve.wait_ge(taken[half], i + (NG_DOWN2 // 2 + 1))
                        for j in range(QD):
                            last = V.tensor_scalar(full[:, half, j, :], xT[:, bass.ds(i * 8 + 4 * half + j, 1), :],
                                                   par[:, bass.ds(i * 8 + (R_PLE + 4 * half + j), 1)], None, ALU.mult)
                            if j == 0:
                                last.then_inc(x_new, 1)
                        last.then_inc(unit_full, 1)
                    if k == half * n + n + 4:
                        earlier()
                        dve.wait_ge(unit_high, i * 2 + (U_X2 + half + 1))
                        q = bass.ds(i * 8 + 4 * half, 4)
                        V.tensor_tensor(h_lo[:, q, :], full[:, half, :, :], h_hi[:, q, :].bitcast(F32), ALU.subtract).then_inc(unit_split, 1)
                    if k == half * n + n + 5:
                        earlier()
                        dve.wait_ge(xsq_ready, i * 2 + (4 + half + 1))
                        fold(sqfold[:], sqx[:]).then_inc(folded, 1)
                        dve.wait_ge(folded, i * 2 + (half + 1))
                        dve.wait_ge(xsum_ready, i * 2 + (4 + half))
                        V.tensor_tensor(sqsum[:], sqsum[:], sqfold[:], ALU.add).then_inc(xsum_ready, 1)
        for c in range(PLEG + 12, END + 5):
            if c < END:
                split(c)
            if PLEG + 12 <= c:
                earlier()
            if c == PLEG + 12:
                dve.wait_ge(xss, 2)
                V.tensor_scalar(ms[:, 0:TT], fa[:, 0, 0:TT], 1.0 / D, EPS, ALU.mult, ALU.add).then_inc(ms_ready, 1)
                dve.wait_ge(rs_ready, 9)
                V.tensor_scalar(small[:, 14:15], ms[:, 0:1], 0.5, None, ALU.mult)
                V.tensor_scalar(small[:, 13:14], ms[:, 1:2], 0.5, None, ALU.mult).then_inc(r2_ready, 1)
            for g in range(3):
                if c == PLEG + 8 * g + (14 if g == 0 else 12):
                    number = NG_PLEG + g
                    cols = slice(g * W, (g + 1) * W)
                    wait_taken(dve, number)
                    dve.wait_ge(x2_taken, g + 1)
                    if g >= 2:
                        dve.wait_ge(out_landed[g % 2], 16 * TT)
                    V.scalar_tensor_tensor(fin[:, g % 2, :, :], gt2[:], 1.0, ple[:, :, cols], ALU.add, ALU.mult).then_inc(pg_ready, 1)
                    dve.wait_ge(pg_ready, g + 1)
                    V.tensor_tensor(fin[:, g % 2, :, :], fin[:, g % 2, :, :], x2tok[:, :, cols], ALU.add).then_inc(out_ready, 1)
        cols = slice(3 * W, 4 * W)
        dve.wait_ge(x2_taken, 4)
        dve.wait_ge(out_landed[1], 16 * TT)
        for t in range(TT):
            dve.wait_ge(tile_gate, t + 1)
            V.scalar_tensor_tensor(fin[:, 1, t, :], gt2[:, t, :], 1.0, ple[:, t, cols], ALU.add, ALU.mult).then_inc(pg_ready, 1)
            dve.wait_ge(pg_ready, 4 + t)
            V.tensor_tensor(fin[:, 1, t, :], fin[:, 1, t, :], x2tok[:, t, cols], ALU.add).then_inc(out_ready, 1)

    block.__exit__(None, None, None)


_INS = ["x", "p", "norm_mix_g", "w_in", "conv_w", "conv_b", "conv_ln_g", "conv_ln_b", "w_conv_out",
        "gla_w_a2", "gla_b_a", "gla_norm_g", "w_gla_out", "moba_q_norm_g", "moba_k_norm_g", "w_moba_out",
        "w_gate", "b_gate", "w_out", "norm_ffn_g", "w_up", "ffn_conv_w", "w_down",
        "norm_ple_g", "w_ple_gate", "w_ple"]


def kernel(**inputs):
    import concourse.bacc as bacc
    from concourse.bass_utils import run_bass_kernel_spmd

    nc = bacc.Bacc("TRN2", target_bir_lowering=False, num_devices=1)
    arrays, args = {}, []
    for name in _INS:
        a = np.ascontiguousarray(inputs[name])
        arrays[f"in_{name}"] = a
        args.append(nc.dram_tensor(f"in_{name}", a.shape, mybir.dt.from_np(a.dtype), kind="ExternalInput").ap())
    out = nc.dram_tensor("out_0", (1, S, D), F32, kind="ExternalOutput").ap()
    trunk(nc, *args, out)
    r = run_bass_kernel_spmd(nc, [arrays], core_ids=[0])
    return r.results[0]["out_0"]
```
